# Optimizing a Trainium2 kernel written in Bass

```python
import math
import jax, jax.numpy as jnp
from jax import lax
import numpy as np

D_MODEL = 2048
BATCH = 1
SEQ = 256
DEPTH = 1

MIX_WIDTH = D_MODEL
ATTN_WIDTH = MIX_WIDTH // 2
SSM_WIDTH = MIX_WIDTH - ATTN_WIDTH
ATTN_HEAD_DIM = 128
ATTN_HEADS = ATTN_WIDTH // ATTN_HEAD_DIM
MOBA_BLOCK = 256
MOBA_TOPK = 3
Q_CHUNK = 32
SSM_HEAD_DIM = 64
SSM_HEADS = SSM_WIDTH // SSM_HEAD_DIM
SSM_GROUPS = 2
SSM_HEADS_PER_GROUP = SSM_HEADS // SSM_GROUPS
SSM_STATE = 128
SSM_CONV = 4
SSD_CHUNK = 128
XBC_WIDTH = SSM_WIDTH + 2 * SSM_GROUPS * SSM_STATE
IN_COLS = 3 * ATTN_WIDTH + SSM_WIDTH + XBC_WIDTH + SSM_HEADS
SPLIT_POINTS = (ATTN_WIDTH, 2 * ATTN_WIDTH, 3 * ATTN_WIDTH,
                3 * ATTN_WIDTH + SSM_WIDTH, 3 * ATTN_WIDTH + SSM_WIDTH + XBC_WIDTH)
D_FF = 5632
FFN_CONV = 3
EPS = 1e-6


def rms_norm(x, w):
    xf = x.astype(jnp.float32)
    y = xf * lax.rsqrt(jnp.mean(xf * xf, axis=-1, keepdims=True) + EPS)
    return (y * w.astype(jnp.float32)).astype(x.dtype)

def causal_dwconv(u, w, bias):
    k_width = w.shape[0]
    s = u.shape[1]
    up = jnp.pad(u, ((0, 0), (k_width - 1, 0), (0, 0)))
    out = bias + up[:, 0:s] * w[0]
    for j in range(1, k_width):
        out = out + up[:, j:j + s] * w[j]
    return out

def moba_attention(q, k, v):
    b, h, s, dh = q.shape
    nb = -(-s // MOBA_BLOCK)
    pad = nb * MOBA_BLOCK - s
    kb = jnp.pad(k, ((0, 0), (0, 0), (0, pad), (0, 0))).reshape(b, h, nb, MOBA_BLOCK, dh)
    vb = jnp.pad(v, ((0, 0), (0, 0), (0, pad), (0, 0))).reshape(b, h, nb, MOBA_BLOCK, dh)
    k_mean = jnp.mean(kb, axis=3)
    n_sel = min(MOBA_TOPK, nb - 1)
    scale = dh ** -0.5
    blk_ids = jnp.arange(nb, dtype=jnp.int32)
    key_off = jnp.arange(MOBA_BLOCK, dtype=jnp.int32)
    gather_blocks = jax.vmap(jax.vmap(lambda blocks, idx: blocks[idx]))
    nq = s // Q_CHUNK
    q_chunks = q.reshape(b, h, nq, Q_CHUNK, dh).transpose(2, 0, 1, 3, 4)

    def chunk_attend(args):
        qc, c = args
        q_pos = c * Q_CHUNK + jnp.arange(Q_CHUNK, dtype=jnp.int32)
        own = (c * Q_CHUNK) // MOBA_BLOCK
        k_own = lax.dynamic_index_in_dim(kb, own, axis=2, keepdims=False)
        v_own = lax.dynamic_index_in_dim(vb, own, axis=2, keepdims=False)
        k_pos = own * MOBA_BLOCK + key_off
        s_own = jnp.einsum('bhqd,bhkd->bhqk', qc, k_own).astype(jnp.float32) * scale
        s_own = jnp.where(k_pos[None, :] <= q_pos[:, None], s_own, -jnp.inf)
        if n_sel == 0:
            p_own = jax.nn.softmax(s_own, axis=-1).astype(v.dtype)
            return jnp.einsum('bhqk,bhkd->bhqd', p_own, v_own)
        gate = jnp.einsum('bhqd,bhnd->bhqn', qc, k_mean).astype(jnp.float32)
        gate = jnp.where(blk_ids < own, gate, -jnp.inf)
        _, sel = lax.top_k(gate, n_sel)
        valid = sel < own
        k_sel = gather_blocks(kb, sel)
        v_sel = gather_blocks(vb, sel)
        s_sel = jnp.einsum('bhqd,bhqjkd->bhqjk', qc, k_sel).astype(jnp.float32) * scale
        s_sel = jnp.where(valid[..., None], s_sel, -jnp.inf).reshape(b, h, Q_CHUNK, n_sel * MOBA_BLOCK)
        p = jax.nn.softmax(jnp.concatenate([s_sel, s_own], axis=-1), axis=-1).astype(v.dtype)
        p_sel = p[..., :n_sel * MOBA_BLOCK].reshape(b, h, Q_CHUNK, n_sel, MOBA_BLOCK)
        p_own = p[..., n_sel * MOBA_BLOCK:]
        return (jnp.einsum('bhqjk,bhqjkd->bhqd', p_sel, v_sel)
                + jnp.einsum('bhqk,bhkd->bhqd', p_own, v_own))

    out = lax.map(chunk_attend, (q_chunks, jnp.arange(nq, dtype=jnp.int32)))
    return out.transpose(1, 2, 0, 3, 4).reshape(b, h, s, dh)

def ssd_chunked_scan(xs, dt, a, bm, cm):
    b, s, g, r, p = xs.shape
    n = bm.shape[-1]
    nc = s // SSD_CHUNK
    L = SSD_CHUNK
    log_a = (dt * a).reshape(b, nc, L, g, r).transpose(0, 3, 4, 1, 2)
    xdt = (xs * dt[..., None]).reshape(b, nc, L, g, r, p)
    bc = bm.reshape(b, nc, L, g, n)
    cc = cm.reshape(b, nc, L, g, n)
    a_cum = jnp.cumsum(log_a, axis=-1)
    tril = jnp.tril(jnp.ones((L, L), dtype=bool))
    seg = a_cum[..., :, None] - a_cum[..., None, :]
    decay = jnp.where(tril, jnp.exp(jnp.where(tril, seg, 0.0)), 0.0)
    cb = jnp.einsum('bclgn,bcsgn->bgcls', cc, bc)
    y_diag = jnp.einsum('bgrcls,bcsgrp->bclgrp', cb[:, :, None] * decay, xdt)
    decay_to_end = jnp.exp(a_cum[..., -1:] - a_cum)
    chunk_states = jnp.einsum('bclgn,bgrcl,bclgrp->cbgrpn', bc, decay_to_end, xdt)
    chunk_decay = jnp.exp(a_cum[..., -1]).transpose(3, 0, 1, 2)

    def carry_state(h, inputs):
        st, dec = inputs
        return h * dec[..., None, None] + st, h

    h0 = jnp.zeros((b, g, r, p, n), xs.dtype)
    _, h_in = lax.scan(carry_state, h0, (chunk_states, chunk_decay))
    y_off = jnp.einsum('bclgn,cbgrpn,bgrcl->bclgrp', cc, h_in, jnp.exp(a_cum))
    return (y_diag + y_off).reshape(b, s, g, r, p)

def hybrid_layer(x, norm1_w, w_in, q_norm_w, k_norm_w, ssm_conv_w, ssm_conv_b, dt_bias, a_log,
                 d_skip, ssm_norm_w, w_out, norm2_w, w_up, ffn_conv_w, ffn_conv_b, w_down):
    b, s, _ = x.shape
    h = rms_norm(x, norm1_w)
    proj = h @ w_in
    q, k, v, z, xbc, dt_raw = jnp.split(proj, SPLIT_POINTS, axis=-1)

    q = rms_norm(q.reshape(b, s, ATTN_HEADS, ATTN_HEAD_DIM), q_norm_w).transpose(0, 2, 1, 3)
    k = rms_norm(k.reshape(b, s, ATTN_HEADS, ATTN_HEAD_DIM), k_norm_w).transpose(0, 2, 1, 3)
    v = v.reshape(b, s, ATTN_HEADS, ATTN_HEAD_DIM).transpose(0, 2, 1, 3)
    attn = moba_attention(q, k, v).transpose(0, 2, 1, 3).reshape(b, s, ATTN_WIDTH)

    xbc = jax.nn.silu(causal_dwconv(xbc, ssm_conv_w, ssm_conv_b))
    xs, bm, cm = jnp.split(xbc, (SSM_WIDTH, SSM_WIDTH + SSM_GROUPS * SSM_STATE), axis=-1)
    xs = xs.astype(jnp.float32).reshape(b, s, SSM_GROUPS, SSM_HEADS_PER_GROUP, SSM_HEAD_DIM)
    bm = bm.astype(jnp.float32).reshape(b, s, SSM_GROUPS, SSM_STATE)
    cm = cm.astype(jnp.float32).reshape(b, s, SSM_GROUPS, SSM_STATE)
    dt = jax.nn.softplus(dt_raw.astype(jnp.float32) + dt_bias.astype(jnp.float32))
    dt = dt.reshape(b, s, SSM_GROUPS, SSM_HEADS_PER_GROUP)
    a = -jnp.exp(a_log.astype(jnp.float32)).reshape(SSM_GROUPS, SSM_HEADS_PER_GROUP)
    y = ssd_chunked_scan(xs, dt, a, bm, cm)
    y = y + d_skip.astype(jnp.float32).reshape(SSM_GROUPS, SSM_HEADS_PER_GROUP)[:, :, None] * xs
    gate = jax.nn.silu(z.astype(jnp.float32)).reshape(b, s, SSM_GROUPS, SSM_HEADS_PER_GROUP * SSM_HEAD_DIM)
    y = y.reshape(b, s, SSM_GROUPS, SSM_HEADS_PER_GROUP * SSM_HEAD_DIM) * gate
    y = rms_norm(y, ssm_norm_w.reshape(SSM_GROUPS, SSM_HEADS_PER_GROUP * SSM_HEAD_DIM))
    ssm = y.reshape(b, s, SSM_WIDTH).astype(x.dtype)

    x = x + jnp.concatenate([attn, ssm], axis=-1) @ w_out

    h = rms_norm(x, norm2_w)
    u = causal_dwconv(h @ w_up, ffn_conv_w, ffn_conv_b)
    u_gate, u_val = jnp.split(u, 2, axis=-1)
    return x + (jax.nn.silu(u_gate) * u_val) @ w_down

def first_inputs(seed: int = 0) -> dict:
    key = jax.random.key(seed)
    ks = jax.random.split(key, 17)

    def nrm(k, shape, scale):
        return jax.random.normal(k, shape, jnp.float32) * scale

    x = nrm(ks[0], (BATCH, SEQ, D_MODEL), 1.0)
    norm1_w = 1.0 + nrm(ks[1], (DEPTH, D_MODEL), 0.02)
    w_in = nrm(ks[2], (DEPTH, D_MODEL, IN_COLS), D_MODEL ** -0.5)
    q_norm_w = 1.0 + nrm(ks[3], (DEPTH, ATTN_HEAD_DIM), 0.02)
    k_norm_w = 1.0 + nrm(ks[4], (DEPTH, ATTN_HEAD_DIM), 0.02)
    ssm_conv_w = nrm(ks[5], (DEPTH, SSM_CONV, XBC_WIDTH), SSM_CONV ** -0.5)
    ssm_conv_b = nrm(ks[6], (DEPTH, XBC_WIDTH), 0.02)
    dt0 = jnp.exp(jax.random.uniform(ks[7], (DEPTH, SSM_HEADS), jnp.float32,
                                     minval=math.log(1e-3), maxval=math.log(1e-1)))
    dt_bias = dt0 + jnp.log(-jnp.expm1(-dt0))
    a_log = jnp.log(jax.random.uniform(ks[8], (DEPTH, SSM_HEADS), jnp.float32, minval=1.0, maxval=16.0))
    d_skip = 1.0 + nrm(ks[9], (DEPTH, SSM_HEADS), 0.1)
    ssm_norm_w = 1.0 + nrm(ks[10], (DEPTH, SSM_WIDTH), 0.02)
    w_out = nrm(ks[11], (DEPTH, MIX_WIDTH, D_MODEL), MIX_WIDTH ** -0.5)
    norm2_w = 1.0 + nrm(ks[12], (DEPTH, D_MODEL), 0.02)
    w_up = nrm(ks[13], (DEPTH, D_MODEL, 2 * D_FF), D_MODEL ** -0.5)
    ffn_conv_w = nrm(ks[14], (DEPTH, FFN_CONV, 2 * D_FF), FFN_CONV ** -0.5)
    ffn_conv_b = nrm(ks[15], (DEPTH, 2 * D_FF), 0.02)
    w_down = nrm(ks[16], (DEPTH, D_FF, D_MODEL), D_FF ** -0.5)
    return {"x": x, "norm1_w": norm1_w, "w_in": w_in, "q_norm_w": q_norm_w, "k_norm_w": k_norm_w,
            "ssm_conv_w": ssm_conv_w, "ssm_conv_b": ssm_conv_b, "dt_bias": dt_bias, "a_log": a_log,
            "d_skip": d_skip, "ssm_norm_w": ssm_norm_w, "w_out": w_out, "norm2_w": norm2_w,
            "w_up": w_up, "ffn_conv_w": ffn_conv_w, "ffn_conv_b": ffn_conv_b, "w_down": w_down}

def first_block(x, norm1_w, w_in, q_norm_w, k_norm_w, ssm_conv_w, ssm_conv_b, dt_bias, a_log,
              d_skip, ssm_norm_w, w_out, norm2_w, w_up, ffn_conv_w, ffn_conv_b, w_down):
    for i in range(DEPTH):
        x = hybrid_layer(x, norm1_w[i], w_in[i], q_norm_w[i], k_norm_w[i], ssm_conv_w[i],
                         ssm_conv_b[i], dt_bias[i], a_log[i], d_skip[i], ssm_norm_w[i], w_out[i],
                         norm2_w[i], w_up[i], ffn_conv_w[i], ffn_conv_b[i], w_down[i])
    return x


ATTN_WIDTH_2 = D_MODEL // 2
HEAD_DIM_ATTN = 128
N_HEADS_ATTN = ATTN_WIDTH_2 // HEAD_DIM_ATTN
DILATION_PATTERNS = ((128, 1), (512, 4), (2048, 16))
RET_WIDTH = D_MODEL // 2
N_HEADS_RET = 4
RET_V_DIM = RET_WIDTH // N_HEADS_RET
RET_QK_DIM = RET_V_DIM // 2
RET_CHUNK = 128
MIX_WIDTH_2 = ATTN_WIDTH_2 + RET_WIDTH
IN_SPLIT_SIZES = (ATTN_WIDTH_2, ATTN_WIDTH_2, ATTN_WIDTH_2, ATTN_WIDTH_2,
                  N_HEADS_RET * RET_QK_DIM, N_HEADS_RET * RET_QK_DIM, RET_WIDTH, RET_WIDTH)
IN_PROJ_WIDTH = sum(IN_SPLIT_SIZES)
IN_SPLIT_IDX = tuple(int(i) for i in np.cumsum(IN_SPLIT_SIZES)[:-1])
NORM_EPS = 1e-6
MASK_VALUE = -1e30


def rms_norm_2(x, g):
    xf = x.astype(jnp.float32)
    y = xf * lax.rsqrt(jnp.mean(xf * xf, axis=-1, keepdims=True) + NORM_EPS)
    return (y * g.astype(jnp.float32)).astype(x.dtype)

def alibi_slopes(n_heads):
    return jnp.exp2(-8.0 * (jnp.arange(n_heads, dtype=jnp.float32) + 1.0) / n_heads)

def dilated_window_attention(q, k, v, window, dilation, slopes):
    b, s, h, e = q.shape
    radius = window // (2 * dilation)
    blk = radius
    sub_len = s // dilation
    n_blk = -(-sub_len // blk)
    pad_len = n_blk * blk
    def to_sub(t):
        return t.reshape(b, sub_len, dilation, h, e)
    qs = jnp.pad(to_sub(q), ((0, 0), (0, pad_len - sub_len), (0, 0), (0, 0), (0, 0)))
    qb = qs.reshape(b, n_blk, blk, dilation, h, e)
    def key_windows(t):
        tp = jnp.pad(to_sub(t), ((0, 0), (blk, blk + pad_len - sub_len), (0, 0), (0, 0), (0, 0)))
        tb = tp.reshape(b, n_blk + 2, blk, dilation, h, e)
        return jnp.concatenate([tb[:, :-2], tb[:, 1:-1], tb[:, 2:]], axis=2)
    kw = key_windows(k)
    vw = key_windows(v)
    scores = jnp.einsum('bnirhe,bnjrhe->bnrhij', qb, kw).astype(jnp.float32)
    i_idx = jnp.arange(blk)[:, None]
    j_idx = jnp.arange(3 * blk)[None, :]
    rel = j_idx - blk - i_idx
    key_pos = jnp.arange(n_blk)[:, None] * blk + jnp.arange(3 * blk)[None, :] - blk
    valid = (key_pos >= 0) & (key_pos < sub_len)
    mask = (jnp.abs(rel) <= radius)[None] & valid[:, None, :]
    dist = (jnp.abs(rel) * dilation).astype(jnp.float32)
    bias = -slopes[:, None, None] * dist[None]
    scores = jnp.where(mask[None, :, None, None], scores + bias[None, None, None], MASK_VALUE)
    m = jnp.max(scores, axis=-1, keepdims=True)
    p = jnp.exp(scores - m)
    den = jnp.sum(p, axis=-1)
    o = jnp.einsum('bnrhij,bnjrhe->bnirhe', p, vw.astype(jnp.float32))
    o = o / den.transpose(0, 1, 4, 2, 3)[..., None]
    lse = (m[..., 0] + jnp.log(den)).transpose(0, 1, 4, 2, 3)
    o = o.reshape(b, pad_len, dilation, h, e)[:, :sub_len].reshape(b, s, h, e)
    lse = lse.reshape(b, pad_len, dilation, h)[:, :sub_len].reshape(b, s, h)
    return o, lse

def dilated_attention_mixture(q, k, v):
    slopes = alibi_slopes(q.shape[2])
    outs, lses = [], []
    for window, dilation in DILATION_PATTERNS:
        o, lse = dilated_window_attention(q, k, v, window, dilation, slopes)
        outs.append(o)
        lses.append(lse)
    w = jax.nn.softmax(jnp.stack(lses, axis=0), axis=0)
    o = jnp.sum(w[..., None] * jnp.stack(outs, axis=0), axis=0)
    return o.astype(v.dtype)

def retention_one_direction(q, k, v, log_gamma):
    b, s, h, dk = q.shape
    dv = v.shape[-1]
    c = RET_CHUNK
    n = s // c
    def chunk(t):
        return t.reshape(b, n, c, h, t.shape[-1]).transpose(1, 0, 3, 2, 4)
    qc, kc, vc = chunk(q), chunk(k), chunk(v)
    idx = jnp.arange(c, dtype=jnp.float32)
    rel = idx[:, None] - idx[None, :]
    lg = log_gamma[:, None, None]
    decay = jnp.where(rel[None] >= 0, jnp.exp(jnp.maximum(rel, 0.0)[None] * lg), 0.0).astype(q.dtype)
    xi = jnp.exp((idx[None] + 1.0) * log_gamma[:, None]).astype(q.dtype)[..., None]
    zeta = jnp.exp((c - 1.0 - idx[None]) * log_gamma[:, None]).astype(q.dtype)[..., None]
    g_chunk = jnp.exp(c * log_gamma).astype(q.dtype)[:, None, None]

    def step(state, inp):
        qi, ki, vi = inp
        inner = jnp.einsum('bhid,bhjd->bhij', qi, ki) * decay
        o = jnp.einsum('bhij,bhje->bhie', inner, vi) + jnp.einsum('bhid,bhde->bhie', qi, state) * xi
        state = state * g_chunk + jnp.einsum('bhjd,bhje->bhde', ki * zeta, vi)
        return state, o

    state0 = jnp.zeros((b, h, dk, dv), dtype=q.dtype)
    _, oc = lax.scan(step, state0, (qc, kc, vc))
    return oc.transpose(1, 0, 3, 2, 4).reshape(b, s, h, dv)

def bidirectional_retention(q, k, v, decay_logit_f, decay_logit_b):
    lg_f = jax.nn.log_sigmoid(decay_logit_f.astype(jnp.float32))
    lg_b = jax.nn.log_sigmoid(decay_logit_b.astype(jnp.float32))
    o_f = retention_one_direction(q, k, v, lg_f)
    o_b = jnp.flip(retention_one_direction(jnp.flip(q, 1), jnp.flip(k, 1), jnp.flip(v, 1), lg_b), 1)
    o = (o_f + o_b).astype(jnp.float32)
    o = o * lax.rsqrt(jnp.mean(o * o, axis=-1, keepdims=True) + NORM_EPS)
    return o.astype(v.dtype)

def hybrid_layer_2(x, c_act, g, w_ada, b_ada, w_in, w_out, dec_f, dec_b):
    b, s, _ = x.shape
    mod = c_act @ w_ada + b_ada
    shift, scale, gate = jnp.split(mod, 3, axis=-1)
    h = rms_norm_2(x, g) * (1.0 + scale[:, None]) + shift[:, None]
    proj = jnp.einsum('bsd,df->bsf', h, w_in)
    q_a, k_a, v_a, z_a, q_r, k_r, v_r, z_r = jnp.split(proj, IN_SPLIT_IDX, axis=-1)
    q_a = q_a.reshape(b, s, N_HEADS_ATTN, HEAD_DIM_ATTN) * (HEAD_DIM_ATTN ** -0.5)
    k_a = k_a.reshape(b, s, N_HEADS_ATTN, HEAD_DIM_ATTN)
    v_a = v_a.reshape(b, s, N_HEADS_ATTN, HEAD_DIM_ATTN)
    y_a = dilated_attention_mixture(q_a, k_a, v_a).reshape(b, s, ATTN_WIDTH_2)
    q_r = q_r.reshape(b, s, N_HEADS_RET, RET_QK_DIM)
    k_r = k_r.reshape(b, s, N_HEADS_RET, RET_QK_DIM) * (RET_QK_DIM ** -0.5)
    v_r = v_r.reshape(b, s, N_HEADS_RET, RET_V_DIM)
    y_r = bidirectional_retention(q_r, k_r, v_r, dec_f, dec_b).reshape(b, s, RET_WIDTH)
    y = jnp.concatenate([y_a * jax.nn.silu(z_a), y_r * jax.nn.silu(z_r)], axis=-1)
    out = jnp.einsum('bsf,fd->bsd', y, w_out)
    return x + gate[:, None] * out

def second_inputs(seed: int = 0) -> dict:
    key = jax.random.key(seed)
    ks = jax.random.split(key, 10)
    f32 = jnp.float32
    x = jax.random.normal(ks[0], (BATCH, SEQ, D_MODEL), f32)
    c = jax.random.normal(ks[1], (BATCH, D_MODEL), f32)
    norm_gain = 1.0 + 0.02 * jax.random.normal(ks[2], (DEPTH, D_MODEL), f32)
    w_ada = 0.5 * D_MODEL ** -0.5 * jax.random.normal(ks[3], (DEPTH, D_MODEL, 3 * D_MODEL), f32)
    b_ada = 0.02 * jax.random.normal(ks[4], (DEPTH, 3 * D_MODEL), f32)
    w_in = D_MODEL ** -0.5 * jax.random.normal(ks[5], (DEPTH, D_MODEL, IN_PROJ_WIDTH), f32)
    w_out = MIX_WIDTH_2 ** -0.5 * jax.random.normal(ks[6], (DEPTH, MIX_WIDTH_2, D_MODEL), f32)
    gamma = 1.0 - jnp.exp2(-5.0 - jnp.arange(N_HEADS_RET, dtype=f32))
    base_logit = jnp.log(gamma) - jnp.log1p(-gamma)
    ret_decay_logit_f = base_logit[None] + 0.1 * jax.random.normal(ks[7], (DEPTH, N_HEADS_RET), f32)
    ret_decay_logit_b = base_logit[None] + 0.1 * jax.random.normal(ks[8], (DEPTH, N_HEADS_RET), f32)
    final_gain = 1.0 + 0.02 * jax.random.normal(ks[9], (D_MODEL,), f32)
    return {"x": x, "c": c, "norm_gain": norm_gain, "w_ada": w_ada, "b_ada": b_ada,
            "w_in": w_in, "w_out": w_out, "ret_decay_logit_f": ret_decay_logit_f,
            "ret_decay_logit_b": ret_decay_logit_b, "final_gain": final_gain}

def second_block(x, c, norm_gain, w_ada, b_ada, w_in, w_out, ret_decay_logit_f, ret_decay_logit_b, final_gain):
    c_act = jax.nn.silu(c)
    h = x
    for layer in range(DEPTH):
        h = hybrid_layer_2(h, c_act, norm_gain[layer], w_ada[layer], b_ada[layer], w_in[layer],
                         w_out[layer], ret_decay_logit_f[layer], ret_decay_logit_b[layer])
    return rms_norm_2(h, final_gain)


def setup_inputs(seed=0):
    out = dict(first_inputs(seed))
    for name, value in second_inputs(seed + 1).items():
        if name != "x":
            out[name + "_2"] = value
    return out


def reference(
    x, norm1_w, w_in, q_norm_w, k_norm_w, ssm_conv_w, ssm_conv_b, dt_bias, a_log, d_skip,
    ssm_norm_w, w_out, norm2_w, w_up, ffn_conv_w, ffn_conv_b, w_down, c_2, norm_gain_2, w_ada_2,
    b_ada_2, w_in_2, w_out_2, ret_decay_logit_f_2, ret_decay_logit_b_2, final_gain_2,
):
    x = first_block(
        x, norm1_w, w_in, q_norm_w, k_norm_w, ssm_conv_w, ssm_conv_b, dt_bias, a_log, d_skip,
        ssm_norm_w, w_out, norm2_w, w_up, ffn_conv_w, ffn_conv_b, w_down,
    )
    return second_block(
        x, c_2, norm_gain_2, w_ada_2, b_ada_2, w_in_2, w_out_2, ret_decay_logit_f_2,
        ret_decay_logit_b_2, final_gain_2,
    )


_drawn_inputs = setup_inputs


def setup_inputs(seed=0):
    import zlib

    import numpy as np

    out = dict(_drawn_inputs(seed))
    spreads = {}
    factors = {'norm1_w': 2.876,
     'q_norm_w': 8.0,
     'k_norm_w': 8.0,
     'ssm_conv_b': 3.1,
     'ssm_norm_w': 4.646,
     'norm2_w': 4.511,
     'ffn_conv_b': 4.483,
     'norm_gain_2': 8.0,
     'b_ada_2': 4.977,
     'ret_decay_logit_f_2': 21.984,
     'final_gain_2': 23.03,
     'ret_decay_logit_b_2': 26.032}
    for name, (base, spread) in spreads.items():
        noise = np.random.default_rng([zlib.crc32(name.encode()), seed]).standard_normal(out[name].shape)
        drawn = base * np.exp(spread * noise) if base else spread * noise
        out[name] = __import__('jax').numpy.asarray(drawn.astype(out[name].dtype))
    for name, factor in factors.items():
        out[name] = (out[name] * factor).astype(out[name].dtype)
    return out
```

```python
from contextlib import ExitStack

import concourse.bass as bass
from concourse import mybir

F32 = mybir.dt.float32
F32R = mybir.dt.float32r
ALU = mybir.AluOpType
ACT = mybir.ActivationFunctionType
AX_X = mybir.AxisListType.X

P = 128
S = 256
D = 2048
DT = D // P
EPS = 1e-6
SCALE = float(P) ** -0.5
HEADS = 8
SSM_HEADS = 16
FF_TILES = 44
FF_GROUPS = FF_TILES // 4
RET_HEADS = 4

RAW = 8
SPLIT = 4
LEAD = 4
B_IN, B_OUT, B_FF = 0, 11, 15
B_IN2 = B_FF + 3 * FF_GROUPS
B_OUT2 = B_IN2 + 14
BLOCKS = B_OUT2 + 4
G_IN, G_OUT, G_FF = 0, 11, 15
G_IN2 = G_FF + 6 * FF_GROUPS
G_OUT2 = G_IN2 + 14

COLS = dict(norm1=16, norm2=16, ssm_norm=8, q_norm=1, k_norm=1, gain2=16, final=16, c=16, b_ada=48,
            d_skip=8, ssm_conv=12 * 5, ffn_conv=88 * 4, dt_bias=16, a_log=16, decay=8, eps=1)
AT, _n = {}, 0
for _k, _w in COLS.items():
    AT[_k] = _n
    _n += _w
N_PARAMS = _n
ADA_CHUNK = 1024
ADA_CHUNKS = 3 * D // ADA_CHUNK


def build(nc, xT, weights, w_dt, w_ada, params, const1, const2, outT):
    ctx = ExitStack()
    with ctx:
        at = [(nc.sbuf_base + 127) // 128 * 128]

        def place(name, shape, dtype=F32, offset=None):
            size = 4
            for n in shape[1:]:
                size *= n
            if offset is None:
                offset = at[0]
                at[0] += (size + 31) // 32 * 32
            t = nc.alloc_sbuf_tensor_at(name, shape, dtype, offset=offset)
            return t, offset + (size + 31) // 32 * 32

        def sem(name):
            return ctx.enter_context(nc.semaphore(name))

        X, _ = place("X", [P, DT, S])
        raw, _ = place("raw", [P, RAW, 1024])
        whi, _ = place("whi", [P, SPLIT, 1024], F32R)
        wlo, _ = place("wlo", [P, SPLIT, 1024], F32R)
        gh, _ = place("gh", [P, DT, S], F32R)
        gl, _ = place("gl", [P, DT, S], F32R)
        prm, _ = place("prm", [P, N_PARAMS])
        cst, _ = place("cst", [P, 3 * P])
        rb, _ = place("rb", [P, S])
        small, _ = place("small", [P, 512])
        modT, _ = place("modT", [P, 48])
        ones, ident, tri = cst[:, 0:P], cst[:, P:2 * P], cst[:, 2 * P:3 * P]
        ada_at = at[0]
        ada_w, _ = place("ada_w", [P, 2, ADA_CHUNK])
        ada_acc, _ = place("ada_acc", [P, ADA_CHUNKS, ADA_CHUNK])
        area = at[0]
        QKVZ, o = place("QKVZ", [P, 32, S], offset=area)
        U, o = place("U", [P, 12, S + 3], offset=o)
        mask, o = place("mask", [P, 2, S], offset=o)
        conv_acc, _ = place("conv_acc", [P, 4, S], offset=o)
        SB1, o = place("SB1", [P, 2, 2, S], offset=o)
        PTS1, o = place("PTS1", [P, 2, 2, S], offset=o)
        VS1, o = place("VS1", [P, 2, 2, P], offset=o)
        assert o <= nc.sbuf_usable_end, (o, nc.sbuf_usable_end)
        SQX1, o = place("SQX1", [P, 2, 4, S], offset=area)
        wdt_f, o = place("wdt_f", [P, DT, 16], offset=o)
        wdt_h, o = place("wdt_h", [P, DT, 16], F32R, offset=o)
        wdt_l, o = place("wdt_l", [P, DT, 16], F32R, offset=o)
        XD, o = place("XD", [P, 2, D // 2], offset=area)
        EM, o = place("EM", [P, 2, 3, P], offset=o)
        CB, o = place("CB", [P, 2, 3, P], offset=o)
        YB, o = place("YB", [P, 2, S], offset=o)
        SQY, o = place("SQY", [P, 4, S], offset=o)
        UG, o = place("UG", [P, 4, S + 2], offset=area)
        UV, o = place("UV", [P, 4, S + 2], offset=o)
        CG, o = place("CG", [P, 4, S], offset=o)
        CV, o = place("CV", [P, 4, S], offset=o)
        ah, o = place("ah", [P, 4, S], F32R, offset=o)
        al, o = place("al", [P, 4, S], F32R, offset=o)
        SQX2, o = place("SQX2", [P, 2, 4, S], offset=o)
        SQX3, o = place("SQX3", [P, 2, 4, S], offset=area)
        TH, o = place("TH", [P, 2, 4, S], offset=o)
        QB, o = place("QB", [P, 56, S], offset=ada_at)
        c2, o = place("c2", [P, 6, 2, S], offset=o)
        DM, o = place("DM", [P, RET_HEADS, 2, S], offset=o)
        SB2, o = place("SB2", [P, 2, 2, S], offset=o)
        PTS2, o = place("PTS2", [P, 2, 2, S], offset=o)
        VS2, o = place("VS2", [P, 2, 2, P], offset=o)
        assert o <= nc.sbuf_usable_end, (o, nc.sbuf_usable_end)
        E12 = SB2
        SQR = c2[:, 0:2, :, :]
        SQX4, _ = place("SQX4", [P, 2, 4, S], offset=ada_at)
        PS = ctx.enter_context(nc.psum_tensor("PS", [P, 8, 512], F32))

        def col(name, i=0, n=1):
            return prm[:, AT[name] + i:AT[name] + i + n]

        def acc_tiles(par):
            return PS[:, 2 * par:2 * par + 2, :].rearrange("p b (t s) -> p (b t) s", t=2)

        s_in = sem("s_in")
        s_raw = [sem(f"s_raw{j}") for j in range(RAW)]
        s_hi = sem("s_hi")
        s_lo = sem("s_lo")
        s_used = sem("s_used")
        s_evac = sem("s_evac")
        s_gh, s_gl = sem("s_gh"), sem("s_gl")
        s_mask, s_wdt, s_c2, s_out = sem("s_mask"), sem("s_wdt"), sem("s_c2"), sem("s_out")
        s_ready = sem("s_ready")
        s_sq, s_sum, s_ss, s_root, s_rb = (sem("s_sq"), sem("s_sum"), sem("s_ss"), sem("s_root"), sem("s_rb"))
        s_dve, s_act = sem("s_dve"), sem("s_act")
        s_base, s_tap, s_silu = sem("s_base"), sem("s_tap"), sem("s_silu")
        s_fbase, s_ftap, s_fsilu, s_prod, s_ah, s_al = (sem("s_fbase"), sem("s_ftap"), sem("s_fsilu"),
                                                       sem("s_prod"), sem("s_ah"), sem("s_al"))
        s_wdth, s_wdtl, s_dtp = sem("s_wdth"), sem("s_wdtl"), sem("s_dtp")
        s_sp, s_spe, s_spl, s_la = sem("s_sp"), sem("s_spe"), sem("s_spl"), sem("s_la")
        s_nsq, s_nr, s_nrt, s_qk = sem("s_nsq"), sem("s_nr"), sem("s_nrt"), sem("s_qk")
        s_vt, s_sc, s_pt, s_pv = sem("s_vt"), sem("s_sc"), sem("s_pt"), sem("s_pv")
        s_vs, s_exp, s_pts, s_ahi, s_alo = sem("s_vs"), sem("s_exp"), sem("s_pts"), sem("s_ahi"), sem("s_alo")
        s_sb, s_nm, s_pn, s_gated = sem("s_sb"), sem("s_nm"), sem("s_pn"), sem("s_gated")
        s_ac, s_at, s_nb, s_cb, s_cbm = sem("s_ac"), sem("s_at"), sem("s_nb"), sem("s_cb"), sem("s_cbm")
        s_xt, s_xd, s_z = sem("s_xt"), sem("s_xd"), sem("s_z")
        s_r, s_e, s_ex, s_m, s_y, s_yo = sem("s_r"), sem("s_e"), sem("s_ex"), sem("s_m"), sem("s_y"), sem("s_yo")
        s_ysq, s_ysum, s_yrt, s_yn = sem("s_ysq"), sem("s_ysum"), sem("s_yrt"), sem("s_yn")
        s_c, s_adaw = sem("s_c"), [sem("s_adaw0"), sem("s_adaw1")]
        s_adam, s_ada, s_mod, s_mt = sem("s_adam"), sem("s_ada"), sem("s_mod"), sem("s_mt")
        s_zs, s_pool = sem("s_zs"), sem("s_pool")
        s_de, s_dm, s_rvt, s_rvs, s_rsc, s_rm, s_ro = (sem("s_de"), sem("s_dm"), sem("s_rvt"), sem("s_rvs"),
                                                      sem("s_rsc"), sem("s_rm"), sem("s_ro"))
        s_rsq, s_rsum, s_rrt, s_ry, s_rhi = sem("s_rsq"), sem("s_rsum"), sem("s_rrt"), sem("s_ry"), sem("s_rhi")
        s_h, s_fin = sem("s_h"), sem("s_fin")

        block = ctx.enter_context(nc.Block())

        @block.sync
        def _(sp):
            with sp.Fori(0, BLOCKS) as i:
                for j in range(RAW):
                    sp.wait_ge(s_lo, i * RAW + j + 1)
                    sp.dma_start(raw[:, j, :], weights[bass.ds(i * RAW + j, 1), :, :].rearrange("a p n -> (a p) n")
                                 ).then_inc(s_raw[j], 16)
            for q in range(4):
                sp.wait_ge(s_fin, 4 * q + 4)
                sp.dma_start(outT[:, 4 * q:4 * q + 4, :], X[:, 4 * q:4 * q + 4, :]).then_inc(s_out, 16)
            sp.wait_ge(s_out, 64)

        @block.gpsimd
        def _(pool):
            def load(i, t):
                pool.dma_start(ada_w[:, t % 2, :],
                               w_ada[bass.ds(i * DT + t, 1), :, :].rearrange("a p n -> (a p) n")
                               ).then_inc(s_adaw[t % 2], 16)

            pool.wait_ge(s_c, 1)
            with pool.Fori(0, ADA_CHUNKS) as i:
                acc = ada_acc[:, bass.ds(i, 1), :].rearrange("p a n -> p (a n)")
                load(i, 0)
                for t in range(DT):
                    if t + 1 < DT:
                        load(i, t + 1)
                    w = ada_w[:, t % 2, :]
                    pool.wait_ge(s_adaw[t % 2], i * (16 * DT // 2) + 16 * (t // 2) + 16)
                    pool.sem_inc(s_pool, 1)
                    pool.tensor_scalar(w, w, small[:, 64 + t:65 + t], None, ALU.mult).then_inc(s_adam, 1)
                    pool.wait_ge(s_adam, i * DT + t + 1)
                    pool.sem_inc(s_pool, 1)
                    if t == 0:
                        pool.tensor_copy(acc, w).then_inc(s_ada, 1)
                    else:
                        pool.tensor_tensor(acc, acc, w, ALU.add).then_inc(s_ada, 1)
                    pool.wait_ge(s_ada, i * DT + t + 1)
                    pool.sem_inc(s_pool, 1)

        @block.scalar
        def _(act):
            links = [0]

            def link(ins):
                links[0] += 1
                ins.then_inc(s_act, 1)
                act.wait_ge(s_act, links[0])

            def split(blk, j):
                blk, j = blk + j // RAW, j % RAW
                act.wait_ge(s_raw[j], blk * 16 + 16)
                act.wait_ge(s_used, blk * RAW + j + 1)
                act.activation(whi[:, j % SPLIT, :], raw[:, j, :], ACT.Copy).then_inc(s_hi, 1)

            def group(blk):
                for j in range(8):
                    split(blk, LEAD + j)

            def squares(k, buf):
                for c in range(4):
                    if c >= 2:
                        act.wait_ge(s_sum, 3 * k + c - 1)
                    act.activation(buf[:, (c > 0) * 1, :, :], X[:, 4 * c:4 * c + 4, :], ACT.Square).then_inc(s_sq, 1)

            def root(k, n):
                act.wait_ge(s_ss, k + 1)
                act.activation(rb[:, :], PS[:, 4, 0:S], ACT.Sqrt, bias=col("eps"), scale=1.0 / n).then_inc(s_root, 1)

            def scaled_hi(base, name):
                for t in range(DT):
                    act.activation(gh[:, t, :], X[:, t, :], ACT.Copy, scale=col(name, t)).then_inc(s_gh, 1)

            act.dma_start(prm[:, :], params).then_inc(s_in, 16)
            act.dma_start(X[:, :, :], xT).then_inc(s_in, 16)
            act.dma_start(cst[:, :], const1[:, 0:3 * P]).then_inc(s_in, 16)
            act.dma_start(mask[:, :, :], const1[:, 3 * P:].rearrange("p (b s) -> p b s", b=2)).then_inc(s_mask, 16)
            act.dma_start(wdt_f[:, :, :], w_dt).then_inc(s_wdt, 16)
            act.wait_ge(s_in, 48)
            act.activation(small[:, 64:80], col("c", 0, 16), ACT.Silu).then_inc(s_c, 1)
            scaled_hi(0, "norm1")
            for j in range(LEAD):
                split(B_IN, j)
            squares(0, SQX1)

            def ssm_base(g):
                act.wait_ge(s_evac, G_IN + g + 3)
                if g:
                    act.wait_ge(s_silu, g)
                for t in range(4):
                    w = 5 * (4 * g + t)
                    act.activation(conv_acc[:, t, :], U[:, 4 * g + t, 3:3 + S], ACT.Identity,
                                   bias=col("ssm_conv", w), scale=col("ssm_conv", w + 4)).then_inc(s_base, 1)

            def ssm_silu(g):
                act.wait_ge(s_tap, 12 * (g + 1))
                act.activation(U[:, 4 * g:4 * g + 4, 3:3 + S], conv_acc[:, :, :], ACT.Silu).then_inc(s_silu, 1)

            group(B_IN)
            root(0, D)
            act.wait_ge(s_wdt, 16)
            act.activation(wdt_h[:, :, :], wdt_f[:, :, :], ACT.Copy).then_inc(s_wdth, 1)
            for g in range(3):
                split(B_IN + g + 1, LEAD)
                ssm_base(g)
                for j in range(1, 4):
                    split(B_IN + g + 1, LEAD + j)
                if g < 2:
                    ssm_silu(g)
                    for j in range(4, 8):
                        split(B_IN + g + 1, LEAD + j)
            ssm_silu(2)
            act.wait_ge(s_sp, 1)
            act.activation(small[:, 128:168], small[:, 80:120], ACT.Exp, scale=-1.0).then_inc(s_spe, 1)
            act.activation(small[:, 168:184], col("a_log", 0, 16), ACT.Exp).then_inc(s_spe, 1)
            act.wait_ge(s_sp, 2)
            act.activation(small[:, 232:272], small[:, 192:232], ACT.Ln).then_inc(s_spl, 1)
            for j in range(4, 8):
                split(B_IN + 3, LEAD + j)
            with act.Fori(0, 7) as i:
                group(i + B_IN + 4)

            def attention(first, SB, PTS, VS):
                def values(h):
                    H = first + h
                    act.wait_ge(s_vt, H + 1)
                    if H >= 2:
                        act.wait_ge(s_pv, H - 1)
                    act.activation(VS[:, h % 2, :, :], PS[:, 2 + h % 2, 0:S].rearrange("p (c d) -> p c d", c=2),
                                   ACT.Copy).then_inc(s_vs, 1)

                def exps(h):
                    H = first + h
                    act.wait_ge(s_nm, H + 1)
                    for b in range(2):
                        k = 2 * (h % 2) + b
                        act.activation(SB[:, h % 2, b, :], SB[:, h % 2, b, :], ACT.Exp, bias=small[:, k:k + 1],
                                       accum_out=small[:, 4 + k:5 + k]).then_inc(s_exp, 1)

                def transposed(h):
                    H = first + h
                    act.wait_ge(s_pt, H + 1)
                    if H >= 2:
                        act.wait_ge(s_pv, H - 1)
                    act.activation(PTS[:, h % 2, :, :], PS[:, 6 + h % 2, :].rearrange("p (c d) -> p c d", c=2),
                                   ACT.Copy).then_inc(s_pts, 1)

                def result(h):
                    H = first + h
                    if first == 0:
                        act.wait_ge(s_pv, H + 1)
                        act.activation(gh[:, h, :], PS[:, h % 2, 0:S], ACT.Copy).then_inc(s_ahi, 1)
                    else:
                        act.wait_ge(s_gated, h + 1)
                        act.activation(gh[:, h, :], QB[:, 24 + h, :], ACT.Copy).then_inc(s_ahi, 1)

                for i in range(HEADS + 1):
                    if i < HEADS:
                        values(i)
                    if i:
                        transposed(i - 1)
                    if i < HEADS:
                        exps(i)
                    if i:
                        result(i - 1)

            act.wait_ge(s_evac, G_IN + 11 + 2)
            act.activation(QKVZ[:, 24:32, :], QKVZ[:, 24:32, :], ACT.Silu).then_inc(s_z, 1)
            def head_squares(h):
                if h >= 2:
                    act.wait_ge(s_nr, h - 1)
                act.activation(PTS1[:, h % 2, :, :], QKVZ[:, h:h + 9:8, :], ACT.Square).then_inc(s_nsq, 1)

            def head_root(h):
                act.wait_ge(s_nr, h + 1)
                if h >= 2:
                    act.wait_ge(s_qk, 2 * h - 2)
                act.activation(SB1[:, h % 2, :, :], PS[:, 4 + h % 2, :].rearrange("p (c d) -> p c d", c=2), ACT.Sqrt,
                               bias=col("eps"), scale=1.0 / P).then_inc(s_nrt, 1)

            for h in range(HEADS + 1):
                if h < HEADS:
                    head_squares(h)
                if h:
                    head_root(h - 1)
            act.wait_ge(s_qk, 2 * HEADS)
            attention(0, SB1, PTS1, VS1)
            act.wait_ge(s_ac, 1)
            act.activation(small[0:16, 256:512], PS[0:16, 5, 0:S], ACT.Copy).then_inc(s_at, 1)
            for h in range(SSM_HEADS):
                act.wait_ge(s_e, 3 * h + 3)
                act.activation(EM[:, h % 2, :, :], EM[:, h % 2, :, :], ACT.Exp).then_inc(s_ex, 1)
            for g in range(2):
                act.wait_ge(s_yo, 8 * g + 8)
                if g:
                    act.wait_ge(s_ysum, g)
                act.activation(SQY[:, :, :], QKVZ[:, 24 + 4 * g:28 + 4 * g, :], ACT.Square).then_inc(s_ysq, 1)
                act.wait_ge(s_ysum, g + 1)
                act.activation(YB[:, g, :], PS[:, 4 + g, 0:S], ACT.Sqrt, bias=col("eps"), scale=1.0 / 512).then_inc(s_yrt, 1)
            for g in range(2):
                act.wait_ge(s_yn, 4 * g + 4)
                act.activation(gh[:, 8 + 4 * g:12 + 4 * g, :], QKVZ[:, 24 + 4 * g:28 + 4 * g, :], ACT.Copy).then_inc(s_gh, 1)
            with act.Fori(0, 4) as i:
                group(i + B_OUT)
            act.wait_ge(s_evac, G_OUT + 4 + 2)
            scaled_hi(0, "norm2")
            squares(1, SQX2)

            def ffn_base(i, val):
                src, dst = (UV, CV) if val else (UG, CG)
                for t in range(4):
                    k = (i * 4 + t + (FF_TILES if val else 0)) * 4 + AT["ffn_conv"]
                    act.activation(dst[:, t, :], src[:, t, 2:2 + S], ACT.Identity, bias=prm[:, bass.ds(k, 1)],
                                   scale=prm[:, bass.ds(k + 3, 1)]).then_inc(s_fbase, 1)

            def ffn_silu(i):
                act.wait_ge(s_ftap, i * 16 + 8)
                act.activation(CG[:, :, :], CG[:, :, :], ACT.Silu).then_inc(s_fsilu, 1)

            def ffn_hi(i):
                act.wait_ge(s_prod, i + 1)
                act.activation(ah[:, :, :], CG[:, :, :], ACT.Copy).then_inc(s_ah, 1)

            group(B_FF)
            root(1, D)
            split(B_FF + 1, LEAD)
            act.wait_ge(s_evac, G_FF + 1 + 2)
            ffn_base(0, False)
            for j in range(1, 8):
                split(B_FF + 1, LEAD + j)
            act.wait_ge(s_evac, G_FF + 2 + 2)
            ffn_base(0, True)
            with act.Fori(1, FF_GROUPS) as i:
                blk = i * 3 + (B_FF - 1)
                grp = i * 6 + (G_FF - 4)
                split(blk, LEAD)
                ffn_silu(i - 1)
                for j in range(1, 4):
                    split(blk, LEAD + j)
                ffn_hi(i - 1)
                for j in range(4, 8):
                    split(blk, LEAD + j)
                split(blk + 1, LEAD)
                act.wait_ge(s_evac, grp + 3)
                ffn_base(i, False)
                for j in range(1, 8):
                    split(blk + 1, LEAD + j)
                split(blk + 2, LEAD)
                act.wait_ge(s_evac, grp + 4)
                ffn_base(i, True)
                for j in range(1, 8):
                    split(blk + 2, LEAD + j)
            ffn_silu(FF_GROUPS - 1)
            ffn_hi(FF_GROUPS - 1)
            group(B_IN2 - 1)
            act.wait_ge(s_evac, G_IN2 + 2)
            squares(2, SQX3)
            root(2, D)
            for c in range(4):
                act.wait_ge(s_h, 4 * c + 4)
                act.activation(gh[:, 4 * c:4 * c + 4, :], TH[:, c % 2, :, :], ACT.Copy).then_inc(s_gh, 1)
            act.dma_start(c2[:, :, :, :], const2).then_inc(s_c2, 16)
            with act.Fori(0, 7) as i:
                for par in range(2):
                    group(i * 2 + (B_IN2 + par))
                    act.wait_ge(s_used, i * 16 + (8 * (B_IN2 + par) + 8 + SPLIT))
                    act.activation(QB[:, bass.ds(i * 8 + 4 * par, 4), :], acc_tiles((G_IN2 + par) % 2),
                                   ACT.Copy).then_inc(s_evac, 1)
            act.wait_ge(s_evac, G_OUT2 + 2)
            act.activation(QB[:, 24:32, :], QB[:, 24:32, :], ACT.Silu).then_inc(s_zs, 1)
            act.activation(QB[:, 48:56, :], QB[:, 48:56, :], ACT.Silu).then_inc(s_zs, 1)
            act.wait_ge(s_c2, 16)
            for r in range(RET_HEADS):
                if r:
                    act.wait_ge(s_dm, r)
                for k in range(2):
                    act.activation(E12[:, k, :, :], c2[:, 2 + k, :, :], ACT.Exp,
                                   scale=small[:, 248 + 4 * k + r:249 + 4 * k + r]).then_inc(s_de, 1)
            attention(HEADS, SB2, PTS2, VS2)
            for r in range(RET_HEADS + 1):
                if r < RET_HEADS:
                    act.wait_ge(s_rvt, r + 1)
                    if r >= 2:
                        act.wait_ge(s_ro, r - 1)
                    act.activation(PTS2[:, r % 2, :, :], PS[:, 2 + r % 2, :].rearrange("p (c d) -> p c d", c=2),
                                   ACT.Copy).then_inc(s_rvs, 1)
                if r:
                    q = r - 1
                    act.wait_ge(s_ro, q + 1)
                    act.activation(SQR[:, q % 2, :, :], PS[:, 6 + q % 2, :].rearrange("p (c d) -> p c d", c=2),
                                   ACT.Square).then_inc(s_rsq, 1)
                    act.wait_ge(s_rsum, q + 1)
                    act.activation(VS2[:, q % 2, :, :], PS[:, q % 2, 0:S].rearrange("p (c d) -> p c d", c=2), ACT.Sqrt,
                                   bias=col("eps"), scale=1.0 / S).then_inc(s_rrt, 1)
                    act.wait_ge(s_ry, 2 * q + 2)
                    act.activation(gh[:, 8 + 2 * q:10 + 2 * q, :], QB[:, 48 + 2 * q:50 + 2 * q, :], ACT.Copy).then_inc(s_rhi, 1)
            for g in range(3):
                group(B_OUT2 + g)
            for j in range(4):
                split(B_OUT2 + 3, LEAD + j)
            act.wait_ge(s_evac, G_OUT2 + 4 + 2)
            squares(3, SQX4)
            root(3, D)

        @block.vector
        def _(dve):
            links = [0]

            def link(ins):
                links[0] += 1
                ins.then_inc(s_dve, 1)
                dve.wait_ge(s_dve, links[0])

            def split(blk, j):
                blk, j = blk + j // RAW, j % RAW
                dve.wait_ge(s_hi, blk * RAW + j + 1)
                dve.tensor_tensor(wlo[:, j % SPLIT, :], raw[:, j, :], whi[:, j % SPLIT, :].bitcast(F32),
                                  ALU.subtract).then_inc(s_lo, 1)

            def group(blk):
                for j in range(8):
                    split(blk, LEAD + j)

            def finished(last, grp):
                dve.wait_ge(s_used, last + 1 + SPLIT)
                dve.wait_ge(s_evac, grp + 2)

            def add_to_x(last, grp, par, first):
                finished(last, grp)
                x = X[:, bass.ds(first, 4), :]
                dve.tensor_tensor(x, acc_tiles(par), x, ALU.add).then_inc(s_evac, 1)

            def scaled_lo(base, name):
                for t in range(DT):
                    dve.wait_ge(s_gh, base + t + 1)
                    dve.scalar_tensor_tensor(gl[:, t, :], X[:, t, :], col(name, t), gh[:, t, :].bitcast(F32),
                                             ALU.mult, ALU.subtract).then_inc(s_gl, 1)

            def sum_chunks(k, buf):
                for c in range(1, 4):
                    dve.wait_ge(s_sq, 4 * k + c + 1)
                    if c > 1:
                        dve.wait_ge(s_sum, 3 * k + c - 1)
                    dve.tensor_tensor(buf[:, 0, :, :], buf[:, 0, :, :], buf[:, 1, :, :], ALU.add).then_inc(s_sum, 1)

            def inverse_root(k):
                dve.wait_ge(s_root, k + 1)
                dve.reciprocal(rb[:, :], rb[:, :]).then_inc(s_rb, 1)

            dve.sem_inc(s_lo, RAW)
            dve.sem_inc(s_evac, 2)
            dve.wait_ge(s_in, 48)
            scaled_lo(0, "norm1")
            for j in range(LEAD):
                split(B_IN, j)
            sum_chunks(0, SQX1)
            dve.memset(U[:, :, 0:3], 0.0).then_inc(s_ready, 1)

            def ssm_evac(g):
                finished(8 * (B_IN + g) + 7, G_IN + g)
                dve.wait_ge(s_rb, 1)
                dve.tensor_tensor(U[:, 4 * g:4 * g + 4, 3:3 + S], acc_tiles((G_IN + g) % 2),
                                  rb[:, :].unsqueeze(1).to_broadcast([P, 4, S]), ALU.mult).then_inc(s_evac, 1)

            def ssm_taps(g, t):
                w = 5 * (4 * g + t)
                dve.wait_ge(s_base, 4 * g + t + 1)
                for k in range(3):
                    if k:
                        dve.wait_ge(s_tap, 12 * g + 3 * t + k)
                    dve.scalar_tensor_tensor(conv_acc[:, t, :], U[:, 4 * g + t, 2 - k:2 - k + S],
                                             col("ssm_conv", w + 3 - k), conv_acc[:, t, :], ALU.mult, ALU.add
                                             ).then_inc(s_tap, 1)

            group(B_IN)
            inverse_root(0)
            ssm_evac(0)
            dve.wait_ge(s_wdth, 1)
            dve.tensor_tensor(wdt_l[:, :, :], wdt_f[:, :, :], wdt_h[:, :, :].bitcast(F32), ALU.subtract).then_inc(s_wdtl, 1)
            dve.wait_ge(s_ready, 1)
            for g in range(3):
                split(B_IN + g + 1, LEAD)
                for j in range(1, 4):
                    split(B_IN + g + 1, LEAD + j)
                    ssm_taps(g, j - 1)
                ssm_taps(g, 3)
                if g < 2:
                    for j in range(4, 8):
                        split(B_IN + g + 1, LEAD + j)
                    ssm_evac(g + 1)
            RAWDT = small[:, 16:56]
            dve.wait_ge(s_dtp, 1)
            link(dve.tensor_copy(small[:, 56:58], PS[:, 6, 0:S].rearrange("p (c m) -> p c m", c=2)[:, :, 0]))
            for c in range(2):
                dve.scalar_tensor_tensor(small[:, 16 + 16 * c:32 + 16 * c], PS[:, 5, 16 * c:16 * c + 16],
                                         small[:, 56 + c:57 + c], col("dt_bias", 0, 16), ALU.mult, ALU.add)
            link(dve.tensor_copy(small[:, 48:56], col("decay", 0, 8)))
            dve.scalar_tensor_tensor(small[:, 80:120], RAWDT, -1.0, RAWDT, ALU.mult, ALU.max).then_inc(s_sp, 1)
            dve.wait_ge(s_spe, 1)
            dve.tensor_scalar(small[:, 192:232], small[:, 128:168], 1.0, None, ALU.add).then_inc(s_sp, 1)
            dve.wait_ge(s_sp, 2)
            link(dve.tensor_scalar(small[:, 80:120], small[:, 192:232], 1.0, None, ALU.is_equal))
            link(dve.scalar_tensor_tensor(small[:, 272:312], small[:, 192:232], -1.0, small[:, 80:120], ALU.add, ALU.add))
            link(dve.reciprocal(small[:, 272:312], small[:, 272:312]))
            dve.wait_ge(s_spl, 1)
            link(dve.tensor_tensor(small[:, 232:272], small[:, 232:272], small[:, 80:120], ALU.add))
            link(dve.tensor_tensor(small[:, 232:272], small[:, 232:272], small[:, 272:312], ALU.mult))
            link(dve.tensor_tensor(small[:, 232:272], small[:, 232:272], small[:, 128:168], ALU.mult))
            dve.scalar_tensor_tensor(small[:, 16:48], small[:, 16:48], 0.0, small[:, 232:264], ALU.max, ALU.add)
            link(dve.scalar_tensor_tensor(small[:, 80:88], small[:, 48:56], 0.0, small[:, 264:272], ALU.min, ALU.subtract))
            link(dve.tensor_copy(small[:, 248:256], small[:, 80:88]))
            dve.wait_ge(s_spe, 2)
            dve.scalar_tensor_tensor(small[:, 88:120].rearrange("p (c h) -> p c h", c=2),
                                     small[:, 16:48].rearrange("p (c h) -> p c h", c=2), -1.0,
                                     small[:, 168:184].unsqueeze(1).to_broadcast([P, 2, 16]), ALU.mult, ALU.mult
                                     ).then_inc(s_la, 1)
            for j in range(4, 8):
                split(B_IN + 3, LEAD + j)

            def qkvz(blk, grp, par, first):
                finished(blk * 8 + 7, grp)
                dve.tensor_tensor(QKVZ[:, bass.ds(first, 4), :], acc_tiles(par),
                                  rb[:, :].unsqueeze(1).to_broadcast([P, 4, S]), ALU.mult).then_inc(s_evac, 1)

            qkvz(B_IN + 3, G_IN + 3, 1, 0)
            for g in range(4, 5):
                group(B_IN + g)
                qkvz(B_IN + g, G_IN + g, g % 2, 4 * (g - 3))
            with dve.Fori(0, 3) as i:
                for k in range(2):
                    group(i * 2 + (B_IN + 5 + k))
                    qkvz(i * 2 + (B_IN + 5 + k), i * 2 + (G_IN + 5 + k), (5 + k) % 2, i * 8 + 8 + 4 * k)

            dve.wait_ge(s_evac, G_IN + 11 + 2)
            for h in range(HEADS):
                dve.wait_ge(s_nrt, h + 1)
                link(dve.reciprocal(SB1[:, h % 2, :, :], SB1[:, h % 2, :, :]))
                for k in range(2):
                    t = QKVZ[:, 8 * k + h, :]
                    dve.scalar_tensor_tensor(t, t, col("k_norm" if k else "q_norm"), SB1[:, h % 2, k, :],
                                             ALU.mult, ALU.mult).then_inc(s_qk, 1)

            def attention(first, SB):
                def scores(h):
                    H = first + h
                    if first:
                        if h >= 2:
                            dve.wait_ge(s_pt, H - 1)
                        link(dve.scalar_tensor_tensor(SB[:, h % 2, :, :], c2[:, 0, :, :], -2.0 ** -(h + 1),
                                                      c2[:, 1, :, :], ALU.mult, ALU.add))
                    dve.wait_ge(s_sc, H + 1)
                    if H >= 2:
                        dve.wait_ge(s_pt, H - 1)
                    dve.scalar_tensor_tensor(SB[:, h % 2, :, :], PS[:, 4 + h % 2, :].rearrange("p (c d) -> p c d", c=2),
                                             SCALE, SB[:, h % 2, :, :] if first else mask[:, :, :],
                                             ALU.mult, ALU.add).then_inc(s_sb, 1)
                    dve.wait_ge(s_sb, H + 1)
                    k = 2 * (h % 2)
                    dve.tensor_reduce(small[:, k:k + 2], SB[:, h % 2, :, :], AX_X, ALU.max, negate=True).then_inc(s_nm, 1)

                def normed(h):
                    H = first + h
                    k = 2 * (h % 2)
                    dve.wait_ge(s_exp, 2 * H + 2)
                    link(dve.reciprocal(small[:, 8 + k:10 + k], small[:, 4 + k:6 + k]))
                    for b in range(2):
                        dve.tensor_scalar(SB[:, h % 2, b, :], SB[:, h % 2, b, :], small[:, 8 + k + b:9 + k + b], None,
                                          ALU.mult).then_inc(s_pn, 1)

                def result(h):
                    H = first + h
                    if first:
                        dve.wait_ge(s_pv, H + 1)
                        z = QB[:, 24 + h, :]
                        dve.tensor_tensor(z, PS[:, h % 2, 0:S], z, ALU.mult).then_inc(s_gated, 1)
                        dve.wait_ge(s_ahi, H + 1)
                        dve.tensor_tensor(gl[:, h, :], z, gh[:, h, :].bitcast(F32), ALU.subtract).then_inc(s_gl, 1)
                    else:
                        dve.wait_ge(s_ahi, H + 1)
                        dve.tensor_tensor(gl[:, h, :], PS[:, h % 2, 0:S], gh[:, h, :].bitcast(F32),
                                          ALU.subtract).then_inc(s_gl, 1)

                for i in range(HEADS + 1):
                    if i < HEADS:
                        scores(i)
                    if i:
                        result(i - 1)
                    if i < HEADS:
                        normed(i)

            dve.wait_ge(s_mask, 16)
            attention(0, SB1)

            NB = small[:, 128:176].rearrange("p (k h) -> p k h", k=3)
            dve.wait_ge(s_ac, 1)
            dve.tensor_scalar(NB[:, 0, :], PS[:, 4, 0:16], -1.0, None, ALU.mult)
            link(dve.tensor_scalar(NB[:, 2, :], PS[:, 4, 16:32], -1.0, None, ALU.mult))
            link(dve.tensor_tensor(NB[:, 1, :], PS[:, 4, 32:48], NB[:, 0, :], ALU.add))
            for g in range(2):
                dve.wait_ge(s_cb, g + 1)
                cb = PS[:, 6 + g, 0:3 * P].rearrange("p (k l) -> p k l", k=3)
                dve.tensor_tensor(CB[:, g, 0:3:2, :], cb[:, 0:3:2, :], tri.unsqueeze(1).to_broadcast([P, 2, P]), ALU.mult
                                  ).then_inc(s_cbm, 1)
                dve.tensor_copy(CB[:, g, 1, :], cb[:, 1, :]).then_inc(s_cbm, 1)
            for j in range(8):
                dve.wait_ge(s_xt, j + 1)
                for c in range(2):
                    dve.tensor_tensor(XD[:, c, P * j:P * j + P].rearrange("p (h d) -> p h d", h=2),
                                      PS[:, j % 2, P * c:P * c + P].rearrange("p (h d) -> p h d", h=2),
                                      small[:, 16 + 16 * c + 2 * j:18 + 16 * c + 2 * j].unsqueeze(2).to_broadcast([P, 2, 64]),
                                      ALU.mult).then_inc(s_xd, 1)
            dve.wait_ge(s_cbm, 4)

            def decay(h):
                dve.wait_ge(s_r, h + 1)
                if h >= 2:
                    dve.wait_ge(s_y, h - 1)
                for k in range(3):
                    lo = P if k else 0
                    dve.tensor_scalar(EM[:, h % 2, k, :], PS[:, 4 + h % 2, lo:lo + P], NB[:, k, h:h + 1], 0.0,
                                      ALU.add, ALU.min).then_inc(s_e, 1)

            def weigh(h):
                dve.wait_ge(s_ex, h + 1)
                dve.tensor_tensor(EM[:, h % 2, :, :], EM[:, h % 2, :, :], CB[:, h // 8, :, :], ALU.mult).then_inc(s_m, 1)

            def ssm_out(j):
                dve.wait_ge(s_y, 2 * j + 2)
                if j == 0:
                    dve.wait_ge(s_z, 1)
                dve.scalar_tensor_tensor(YB[:, j % 2, :], U[:, j, 3:3 + S], col("d_skip", j), PS[:, 2 + j % 2, 0:S],
                                         ALU.mult, ALU.add).then_inc(s_yo, 1)
                dve.wait_ge(s_yo, 2 * j + 1)
                dve.tensor_tensor(QKVZ[:, 24 + j, :], YB[:, j % 2, :], QKVZ[:, 24 + j, :], ALU.mult).then_inc(s_yo, 1)

            for h in range(SSM_HEADS + 2):
                if h < SSM_HEADS:
                    decay(h)
                if 1 <= h <= SSM_HEADS:
                    weigh(h - 1)
                if h >= 3 and h % 2 == 1:
                    ssm_out((h - 3) // 2)
            for g in range(2):
                dve.wait_ge(s_yrt, g + 1)
                link(dve.reciprocal(YB[:, g, :], YB[:, g, :]))
                for t in range(4):
                    y = QKVZ[:, 24 + 4 * g + t, :]
                    dve.scalar_tensor_tensor(y, y, col("ssm_norm", 4 * g + t), YB[:, g, :], ALU.mult, ALU.mult
                                             ).then_inc(s_yn, 1)
            for g in range(2):
                dve.wait_ge(s_gh, DT + g + 1)
                dve.tensor_tensor(gl[:, 8 + 4 * g:12 + 4 * g, :], QKVZ[:, 24 + 4 * g:28 + 4 * g, :],
                                  gh[:, 8 + 4 * g:12 + 4 * g, :].bitcast(F32), ALU.subtract).then_inc(s_gl, 1)
            with dve.Fori(0, 2) as i:
                for k in range(2):
                    group(i * 2 + (B_OUT + k))
                    add_to_x(i * 16 + (8 * (B_OUT + k) + 7), i * 2 + (G_OUT + k), (G_OUT + k) % 2, i * 8 + 4 * k)
            dve.wait_ge(s_evac, G_OUT + 4 + 2)
            scaled_lo(DT + 2, "norm2")
            sum_chunks(1, SQX2)
            dve.memset(UG[:, :, 0:2], 0.0).then_inc(s_ready, 1)
            dve.memset(UV[:, :, 0:2], 0.0).then_inc(s_ready, 1)

            def ffn_evac(last, grp, par, dst):
                finished(last, grp)
                dve.tensor_tensor(dst[:, :, 2:2 + S], acc_tiles(par), rb[:, :].unsqueeze(1).to_broadcast([P, 4, S]),
                                  ALU.mult).then_inc(s_evac, 1)

            def ffn_taps(i, val, t):
                src, dst = (UV, CV) if val else (UG, CG)
                k = (i * 4 + t + (FF_TILES if val else 0)) * 4 + AT["ffn_conv"]
                n = 4 if val else 0
                dve.wait_ge(s_fbase, i * 8 + (n + t + 1))
                dve.scalar_tensor_tensor(dst[:, t, :], src[:, t, 1:1 + S], prm[:, bass.ds(k + 2, 1)], dst[:, t, :],
                                         ALU.mult, ALU.add).then_inc(s_ftap, 1)
                dve.wait_ge(s_ftap, i * 16 + (2 * (n + t) + 1))
                dve.scalar_tensor_tensor(dst[:, t, :], src[:, t, 0:S], prm[:, bass.ds(k + 1, 1)], dst[:, t, :],
                                         ALU.mult, ALU.add).then_inc(s_ftap, 1)

            def ffn_product(i):
                dve.wait_ge(s_fsilu, i + 1)
                dve.wait_ge(s_ftap, i * 16 + 16)
                dve.tensor_tensor(CG[:, :, :], CG[:, :, :], CV[:, :, :], ALU.mult).then_inc(s_prod, 1)

            def ffn_lo(i):
                dve.wait_ge(s_ah, i + 1)
                dve.tensor_tensor(al[:, :, :], CG[:, :, :], ah[:, :, :].bitcast(F32), ALU.subtract).then_inc(s_al, 1)

            group(B_FF)
            inverse_root(1)
            dve.wait_ge(s_rb, 2)
            dve.wait_ge(s_ready, 3)
            ffn_evac(8 * B_FF + 7, G_FF, G_FF % 2, UG)
            split(B_FF + 1, LEAD)
            for j in range(1, 8):
                split(B_FF + 1, LEAD + j)
                if 2 <= j < 6:
                    ffn_taps(0, False, j - 2)
            ffn_evac(8 * B_FF + 15, G_FF + 1, (G_FF + 1) % 2, UV)
            for t in range(4):
                ffn_taps(0, True, t)
            with dve.Fori(1, FF_GROUPS) as i:
                blk = i * 3 + (B_FF - 1)
                unit = i * 24 + 8 * (B_FF - 1)
                grp = i * 6 + (G_FF - 4)
                for j in range(8):
                    split(blk, LEAD + j)
                    if j == 1:
                        ffn_product(i - 1)
                    if j == 5:
                        ffn_lo(i - 1)
                ffn_evac(unit + 7, grp, G_FF % 2, UG)
                for j in range(8):
                    split(blk + 1, LEAD + j)
                    if 2 <= j < 6:
                        ffn_taps(i, False, j - 2)
                ffn_evac(unit + 15, grp + 1, (G_FF + 1) % 2, UV)
                for j in range(8):
                    split(blk + 2, LEAD + j)
                    if j % 2:
                        add_to_x(unit + (16 + j), grp + (2 + j // 2), (G_FF + j // 2) % 2, 4 * (j // 2))
                    if 2 <= j < 6:
                        ffn_taps(i, True, j - 2)
            ffn_product(FF_GROUPS - 1)
            ffn_lo(FF_GROUPS - 1)
            dve.wait_ge(s_mod, 1)
            link(dve.tensor_tensor(modT[:, :], PS[:, 5, 0:48], col("b_ada", 0, 48), ALU.add))
            dve.scalar_tensor_tensor(modT[:, 16:32], modT[:, 16:32], 1.0, col("gain2", 0, 16), ALU.add, ALU.mult
                                     ).then_inc(s_mt, 1)
            for d in range(4):
                split(B_IN2 - 1, LEAD + 2 * d)
                split(B_IN2 - 1, LEAD + 2 * d + 1)
                add_to_x(8 * (B_IN2 - 1) + 2 * d + 1, G_IN2 - 4 + d, (G_IN2 - 4 + d) % 2, 4 * d)
            dve.wait_ge(s_evac, G_IN2 + 2)
            sum_chunks(2, SQX3)
            inverse_root(2)
            dve.wait_ge(s_mt, 1)
            for c in range(4):
                if c == 0:
                    dve.wait_ge(s_rb, 3)
                if c >= 2:
                    dve.wait_ge(s_gl, 2 * DT + 10 + c - 1)
                link(dve.tensor_tensor(TH[:, c % 2, :, :], X[:, 4 * c:4 * c + 4, :],
                                       rb[:, :].unsqueeze(1).to_broadcast([P, 4, S]), ALU.mult))
                for t in range(4):
                    k = 4 * c + t
                    h = TH[:, c % 2, t, :]
                    dve.tensor_scalar(h, h, modT[:, 16 + k:17 + k], modT[:, k:k + 1], ALU.mult, ALU.add).then_inc(s_h, 1)
                dve.wait_ge(s_gh, 2 * DT + 2 + c + 1)
                dve.tensor_tensor(gl[:, 4 * c:4 * c + 4, :], TH[:, c % 2, :, :], gh[:, 4 * c:4 * c + 4, :].bitcast(F32),
                                  ALU.subtract).then_inc(s_gl, 1)
            with dve.Fori(0, 14) as i:
                group(i + B_IN2)
            dve.wait_ge(s_c2, 16)
            for r in range(RET_HEADS):
                dve.wait_ge(s_de, 2 * r + 2)
                for k in range(2):
                    dve.tensor_tensor(E12[:, k, :, :], E12[:, k, :, :], c2[:, 4 + k, :, :], ALU.mult).then_inc(s_dve, 1)
                links[0] += 2
                dve.wait_ge(s_dve, links[0])
                dve.tensor_tensor(DM[:, r, :, :], E12[:, 0, :, :], E12[:, 1, :, :], ALU.add).then_inc(s_dm, 1)
            dve.wait_ge(s_zs, 2)
            dve.wait_ge(s_dm, RET_HEADS)
            attention(HEADS, SB2)

            def decayed(r):
                dve.wait_ge(s_rsc, r + 1)
                if r >= 2:
                    dve.wait_ge(s_ro, r - 1)
                if r == 0:
                    dve.wait_ge(s_dm, RET_HEADS)
                dve.scalar_tensor_tensor(SB2[:, r % 2, :, :], PS[:, 4 + r % 2, :].rearrange("p (c d) -> p c d", c=2),
                                         SCALE, DM[:, r, :, :], ALU.mult, ALU.mult).then_inc(s_rm, 1)

            def gated(r):
                dve.wait_ge(s_rrt, r + 1)
                link(dve.reciprocal(VS2[:, r % 2, :, :], VS2[:, r % 2, :, :]))
                o = PS[:, 6 + r % 2, :].rearrange("p (c d) -> p c d", c=2)
                inv = VS2[:, r % 2, :, :].rearrange("p c d -> p (c d)").unsqueeze(1).to_broadcast([P, 2, S])
                z = QB[:, 48 + 2 * r:50 + 2 * r, :]
                dve.tensor_tensor(z, o, z, ALU.mult).then_inc(s_ry, 1)
                dve.wait_ge(s_ry, 2 * r + 1)
                dve.tensor_tensor(z, z, inv, ALU.mult).then_inc(s_ry, 1)
                dve.wait_ge(s_rhi, r + 1)
                dve.tensor_tensor(gl[:, 8 + 2 * r:10 + 2 * r, :], z, gh[:, 8 + 2 * r:10 + 2 * r, :].bitcast(F32),
                                  ALU.subtract).then_inc(s_gl, 1)

            for r in range(RET_HEADS + 1):
                if r < RET_HEADS:
                    decayed(r)
                if r:
                    gated(r - 1)
            for g in range(4):
                for j in range(8 if g < 3 else 4):
                    split(B_OUT2 + g, LEAD + j)
                finished(8 * (B_OUT2 + g) + 7, G_OUT2 + g)
                for t in range(4):
                    k = 4 * g + t
                    ins = dve.scalar_tensor_tensor(X[:, k, :], acc_tiles((G_OUT2 + g) % 2)[:, t, :],
                                                   modT[:, 32 + k:33 + k], X[:, k, :], ALU.mult, ALU.add)
                    if t < 3:
                        links[0] += 1
                        ins.then_inc(s_dve, 1)
                    else:
                        dve.wait_ge(s_dve, links[0])
                        ins.then_inc(s_evac, 1)
            dve.wait_ge(s_evac, G_OUT2 + 4 + 2)
            sum_chunks(3, SQX4)
            inverse_root(3)
            dve.wait_ge(s_rb, 4)
            for t in range(DT):
                dve.scalar_tensor_tensor(X[:, t, :], X[:, t, :], col("final", t), rb[:, :], ALU.mult, ALU.mult
                                         ).then_inc(s_fin, 1)

        @block.tensor
        def _(pe):
            def group(unit, j0, units, grp, par, hi, lo, need):
                pe.wait_ge(s_evac, grp + 1)
                out = acc_tiles(par)
                for u in range(units):
                    b = (j0 + u) % SPLIT
                    pe.wait_ge(s_lo, unit + (u + 1 + RAW))
                    if need is not None:
                        pe.wait_ge(s_gl, need(2 * u + 1))
                    for half in range(2):
                        kt = 2 * u + half
                        first, last = kt == 0, kt == 2 * units - 1
                        for t in range(4):
                            w = slice(512 * half + P * t, 512 * half + P * t + P)
                            pe.matmul(out[:, t, :], whi[:, b, w], hi[:, kt, :], start=first and t % 2 == 0, stop=False,
                                      skip_group_check=True)
                            pe.matmul(out[:, t, :], whi[:, b, w], lo[:, kt, :], start=False, stop=False,
                                      skip_group_check=True)
                            mm = pe.matmul(out[:, t, :], wlo[:, b, w], hi[:, kt, :], start=False, stop=last,
                                           skip_group_check=True)
                    mm.then_inc(s_used, 1)

            def whole(blk, grp, par, need):
                group(blk * 8, 0, 8, grp, par, gh, gl, need)

            def sum_squares(k, buf):
                pe.wait_ge(s_sum, 3 * k + 3)
                if k:
                    pe.wait_ge(s_root, k)
                for t in range(4):
                    mm = pe.matmul(PS[:, 4, 0:S], ones, buf[:, 0, t, :], start=(t == 0), stop=(t == 3))
                mm.then_inc(s_ss, 1)

            pe.sem_inc(s_used, SPLIT)
            pe.wait_ge(s_in, 48)
            need = lambda kt: kt + 1
            whole(B_IN, G_IN, 0, need)
            sum_squares(0, SQX1)
            whole(B_IN + 1, G_IN + 1, 1, need)
            pe.wait_ge(s_wdtl, 1)
            for c in range(2):
                o = PS[:, 5, 16 * c:16 * c + 16]
                for kt in range(DT):
                    x_hi, x_lo = gh[:, kt, P * c:P * c + P], gl[:, kt, P * c:P * c + P]
                    pe.matmul(o, x_hi, wdt_h[:, kt, :], start=(kt == 0), stop=False)
                    pe.matmul(o, x_hi, wdt_l[:, kt, :], start=False, stop=False)
                    pe.matmul(o, x_lo, wdt_h[:, kt, :], start=False, stop=(kt == DT - 1))
            pe.wait_ge(s_rb, 1)
            for c in range(2):
                mm = pe.transpose(PS[:, 6, P * c:P * c + P], rb[:, P * c:P * c + P], ident)
            mm.then_inc(s_dtp, 1)
            whole(B_IN + 2, G_IN + 2, 0, need)
            whole(B_IN + 3, G_IN + 3, 1, need)
            whole(B_IN + 4, G_IN + 4, 0, need)
            with pe.Fori(0, 3) as i:
                for k in range(2):
                    whole(i * 2 + (B_IN + 5 + k), i * 2 + (G_IN + 5 + k), (5 + k) % 2, need)

            pe.wait_ge(s_evac, G_IN + 11 + 2)
            for h in range(HEADS):
                pe.wait_ge(s_nsq, h + 1)
                if h >= 2:
                    pe.wait_ge(s_nrt, h - 1)
                pe.matmul(PS[:, 4 + h % 2, :], ones, PTS1[:, h % 2, :, :], start=True, stop=True).then_inc(s_nr, 1)
            pe.wait_ge(s_nrt, HEADS)

            def attention(first, Q, K, V, SB, PTS, VS):
                for i in range(HEADS + 1):
                    if i < HEADS:
                        h, H = i, first + i
                        if H >= 2:
                            pe.wait_ge(s_vs, H - 1)
                        for c in range(2):
                            mm = pe.transpose(PS[:, 2 + h % 2, P * c:P * c + P], V(h)[:, P * c:P * c + P], ident)
                        mm.then_inc(s_vt, 1)
                        if first == 0:
                            pe.wait_ge(s_qk, 2 * h + 2)
                        if H >= 2:
                            pe.wait_ge(s_sb, H - 1)
                        for c in range(2):
                            mm = pe.matmul(PS[:, 4 + h % 2, S * c:S * c + S], Q(h)[:, P * c:P * c + P], K(h),
                                           start=True, stop=True)
                        mm.then_inc(s_sc, 1)
                    if i:
                        h, H = i - 1, first + i - 1
                        pe.wait_ge(s_pn, 2 * H + 2)
                        if H >= 2:
                            pe.wait_ge(s_pts, H - 1)
                        for c in range(2):
                            for k in range(2):
                                mm = pe.transpose(PS[:, 6 + h % 2, S * k + P * c:S * k + P * c + P],
                                                  SB[:, h % 2, c, P * k:P * k + P], ident)
                        mm.then_inc(s_pt, 1)
                        pe.wait_ge(s_pts, H + 1)
                        pe.wait_ge(s_vs, H + 1)
                        if h >= 2:
                            pe.wait_ge(s_gl, (DT if first == 0 else 2 * DT + 14) + h - 1)
                        for k in range(2):
                            mm = pe.matmul(PS[:, h % 2, 0:S], VS[:, h % 2, k, :], PTS[:, h % 2, k, :],
                                           start=(k == 0), stop=(k == 1))
                        mm.then_inc(s_pv, 1)

            tile = lambda buf, k: (lambda h: buf[:, k + h, :])
            attention(0, tile(QKVZ, 0), tile(QKVZ, 8), tile(QKVZ, 16), SB1, PTS1, VS1)

            LA = small[:, 88:120].rearrange("p (c h) -> p c h", c=2)
            pe.wait_ge(s_la, 1)
            pe.wait_ge(s_silu, 3)
            pe.wait_ge(s_gl, DT + HEADS)
            for c in range(2):
                pe.matmul(PS[:, 4, 16 * c:16 * c + 16], tri, LA[:, c, :], start=True, stop=True)
            pe.matmul(PS[:, 4, 32:48], ones, LA[:, 0, :], start=True, stop=True)
            for c in range(2):
                mm = pe.matmul(PS[0:16, 5, P * c:P * c + P], LA[:, c, :], tri, start=True, stop=True)
            mm.then_inc(s_ac, 1)
            for g in range(2):
                bm, cm = U[:, 8 + g, 3:3 + S], U[:, 10 + g, 3:3 + S]
                pe.matmul(PS[:, 6 + g, 0:S], bm[:, 0:P], cm, start=True, stop=True)
                pe.matmul(PS[:, 6 + g, S:S + P], bm[:, P:S], cm[:, P:S], start=True, stop=True).then_inc(s_cb, 1)
            for j in range(8):
                if j >= 2:
                    pe.wait_ge(s_xd, 2 * j - 2)
                for c in range(2):
                    mm = pe.transpose(PS[:, j % 2, P * c:P * c + P], U[:, j, 3 + P * c:3 + P * c + P], ident)
                mm.then_inc(s_xt, 1)
            pe.wait_ge(s_at, 1)
            pe.wait_ge(s_cbm, 4)
            for h in range(SSM_HEADS + 1):
                if h < SSM_HEADS:
                    if h >= 2:
                        pe.wait_ge(s_e, 3 * h - 3)
                    pe.matmul(PS[:, 4 + h % 2, 0:S], ident[0:16, h:h + 1].to_broadcast([16, P]), small[0:16, 256:512],
                              start=True, stop=True).then_inc(s_r, 1)
                if h:
                    q = h - 1
                    lo, bank = 64 * (q % 2), 2 + q // 2 % 2
                    pe.wait_ge(s_m, q + 1)
                    if q == 0:
                        pe.wait_ge(s_xd, 16)
                    if q >= 4:
                        pe.wait_ge(s_yo, 2 * (q // 2 - 2) + 1)
                    pe.matmul(PS[lo:lo + 64, bank, 0:S], XD[:, 0, 64 * q:64 * q + 64], EM[:, q % 2, 0:2, :],
                              start=True, stop=False, skip_group_check=True)
                    pe.matmul(PS[lo:lo + 64, bank, P:S], XD[:, 1, 64 * q:64 * q + 64], EM[:, q % 2, 2, :],
                              start=False, stop=True, skip_group_check=True).then_inc(s_y, 1)
            for g in range(2):
                pe.wait_ge(s_ysq, g + 1)
                for t in range(4):
                    mm = pe.matmul(PS[:, 4 + g, 0:S], ones, SQY[:, t, :], start=(t == 0), stop=(t == 3))
                mm.then_inc(s_ysum, 1)
            need_out = lambda kt: DT + (kt + 1 if kt < 8 else 9 + (kt - 8) // 4)
            with pe.Fori(0, 2) as i:
                for k in range(2):
                    whole(i * 2 + (B_OUT + k), i * 2 + (G_OUT + k), (G_OUT + k) % 2, need_out)
            need_ff = lambda kt: DT + 10 + kt + 1
            whole(B_FF, G_FF, G_FF % 2, need_ff)
            sum_squares(1, SQX2)
            whole(B_FF + 1, G_FF + 1, (G_FF + 1) % 2, need_ff)

            def down(i, unit, grp):
                pe.wait_ge(s_al, i + 1)
                for d in range(4):
                    group(unit + 2 * d, 2 * d, 2, grp + d, (G_FF + d) % 2, ah, al, None)

            with pe.Fori(1, FF_GROUPS) as i:
                whole(i * 3 + (B_FF - 1), i * 6 + (G_FF - 4), G_FF % 2, need_ff)
                whole(i * 3 + B_FF, i * 6 + (G_FF - 3), (G_FF + 1) % 2, need_ff)
                down(i - 1, i * 24 + 8 * (B_FF + 1), i * 6 + (G_FF - 2))
            pe.wait_ge(s_ada, ADA_CHUNKS * DT)
            for j in range(48):
                mm = pe.matmul(PS[:, 5, j:j + 1], ada_acc[:, P * j // ADA_CHUNK, P * j % ADA_CHUNK:P * j % ADA_CHUNK + P],
                               ones[:, 0:1], start=True, stop=True)
            mm.then_inc(s_mod, 1)
            down(FF_GROUPS - 1, 8 * (B_IN2 - 1), G_IN2 - 4)
            sum_squares(2, SQX3)
            need_in2 = lambda kt: 2 * DT + 10 + kt // 4 + 1
            with pe.Fori(0, 7) as i:
                for k in range(2):
                    whole(i * 2 + (B_IN2 + k), i * 2 + (G_IN2 + k), (G_IN2 + k) % 2, need_in2)
            pe.wait_ge(s_evac, G_OUT2 + 2)
            attention(HEADS, tile(QB, 0), tile(QB, 8), tile(QB, 16), SB2, PTS2, VS2)

            pe.wait_ge(s_gl, 2 * DT + 14 + HEADS)
            for r in range(RET_HEADS + 1):
                if r < RET_HEADS:
                    if r >= 2:
                        pe.wait_ge(s_rvs, r - 1)
                    for c in range(2):
                        for e in range(2):
                            mm = pe.transpose(PS[:, 2 + r % 2, S * c + P * e:S * c + P * e + P],
                                              QB[:, 40 + 2 * r + e, P * c:P * c + P], ident)
                    mm.then_inc(s_rvt, 1)
                    if r >= 2:
                        pe.wait_ge(s_rm, r - 1)
                    for c in range(2):
                        mm = pe.matmul(PS[:, 4 + r % 2, S * c:S * c + S], QB[:, 36 + r, P * c:P * c + P], QB[:, 32 + r, :],
                                       start=True, stop=True)
                    mm.then_inc(s_rsc, 1)
                    pe.wait_ge(s_rm, r + 1)
                    pe.wait_ge(s_rvs, r + 1)
                    if r >= 2:
                        pe.wait_ge(s_ry, 2 * r - 3)
                    for e in range(2):
                        for c in range(2):
                            mm = pe.matmul(PS[:, 6 + r % 2, S * e:S * e + S], PTS2[:, r % 2, c, P * e:P * e + P],
                                           SB2[:, r % 2, c, :], start=(c == 0), stop=(c == 1))
                    mm.then_inc(s_ro, 1)
                if r:
                    q = r - 1
                    pe.wait_ge(s_rsq, q + 1)
                    if q >= 2:
                        pe.wait_ge(s_rrt, q - 1)
                    for e in range(2):
                        mm = pe.matmul(PS[:, q % 2, 0:S], ones, SQR[:, q % 2, e, :], start=(e == 0), stop=(e == 1))
                    mm.then_inc(s_rsum, 1)
            pe.wait_ge(s_rrt, RET_HEADS)
            base = 2 * DT + 14
            need_out2 = lambda kt: base + (kt + 1 if kt < 8 else 9 + (kt - 8) // 2)
            for g in range(4):
                whole(B_OUT2 + g, G_OUT2 + g, (G_OUT2 + g) % 2, need_out2)
            sum_squares(3, SQX4)


def _units(w):
    k, n = w.shape
    return w.reshape(k // 256, 2, P, n // 512, 512).transpose(3, 0, 2, 1, 4).reshape(n // 512, k // 256, P, 1024)


def _cols(v):
    return v.reshape(-1, P).T


def kernel(**inputs):
    import numpy as np
    import concourse.bacc as bacc
    from concourse.bass_utils import run_bass_kernel_spmd

    a = {k: np.asarray(v) for k, v in inputs.items()}
    f = np.float32
    w_in = a["w_in"][0]
    gates = _units(a["w_up"][0])
    downs = _units(a["w_down"][0])
    parts = [_units(w_in[:, 4096:5632]), _units(w_in[:, :4096]), _units(a["w_out"][0])]
    for i in range(FF_GROUPS + 1):
        if i < FF_GROUPS:
            parts += [gates[i], gates[FF_GROUPS + i]]
        if i:
            parts.append(downs[:, 2 * i - 2:2 * i])
    parts += [_units(a["w_in_2"][0]), _units(a["w_out_2"][0])]
    weights = np.concatenate([p.reshape(-1, P, 1024) for p in parts])
    assert len(weights) == BLOCKS * RAW
    w_dt = w_in[:, 5632:].reshape(DT, P, 16).transpose(1, 0, 2)
    w_ada = a["w_ada_2"][0].reshape(DT, P, ADA_CHUNKS, ADA_CHUNK).transpose(2, 0, 1, 3).reshape(-1, P, ADA_CHUNK)

    def rows(v):
        return np.broadcast_to(v.reshape(1, -1), (P, v.size))

    ssm_conv = np.stack([_cols(a["ssm_conv_b"][0])] + [_cols(w) for w in a["ssm_conv_w"][0]], axis=2).reshape(P, -1)
    ffn_conv = np.stack([_cols(a["ffn_conv_b"][0])] + [_cols(w) for w in a["ffn_conv_w"][0]], axis=2).reshape(P, -1)
    table = dict(norm1=_cols(a["norm1_w"][0]), norm2=_cols(a["norm2_w"][0]), ssm_norm=_cols(a["ssm_norm_w"][0]),
                 q_norm=_cols(a["q_norm_w"][0]), k_norm=_cols(a["k_norm_w"][0]), gain2=_cols(a["norm_gain_2"][0]),
                 final=_cols(a["final_gain_2"]), c=_cols(a["c_2"][0]), b_ada=_cols(a["b_ada_2"][0]),
                 d_skip=_cols(np.repeat(a["d_skip"][0], 64)), ssm_conv=ssm_conv, ffn_conv=ffn_conv,
                 dt_bias=rows(a["dt_bias"][0]), a_log=rows(a["a_log"][0]),
                 decay=np.concatenate([rows(a["ret_decay_logit_f_2"][0]), rows(a["ret_decay_logit_b_2"][0])], axis=1),
                 eps=np.full((P, 1), EPS, f))
    params = np.concatenate([table[k] for k in COLS], axis=1)
    xT = a["x"][0].T.reshape(DT, P, S).transpose(1, 0, 2)
    i, j = np.arange(P)[:, None], np.arange(P)[None, :]
    row = (np.arange(P)[:, None, None] + P * np.arange(2)[None, :, None])
    column = np.arange(S)[None, None, :]
    causal = np.where(column <= row, 0.0, -3e38)
    const1 = np.concatenate([np.ones((P, P)), i == j, i <= j, causal.reshape(P, -1)], axis=1).astype(f)
    dist = np.abs(row - column)
    windows = (dist <= 64) * 1 + (dist % 4 == 0) + (dist % 16 == 0)
    log_windows = np.where(windows > 0, np.log(np.maximum(windows, 1)), -1e30)
    behind, ahead = np.maximum(column - row, 0), np.maximum(row - column, 0)
    const2 = np.stack([dist, log_windows, behind, ahead, column >= row, column <= row], axis=1).astype(f)

    nc = bacc.Bacc("TRN2", target_bir_lowering=False, num_devices=1)
    arrays, args = {}, []
    for name, v in dict(xT=xT, weights=weights, w_dt=w_dt, w_ada=w_ada, params=params, const1=const1,
                        const2=const2).items():
        arrays[name] = np.ascontiguousarray(v)
        args.append(nc.dram_tensor(name, v.shape, mybir.dt.from_np(arrays[name].dtype), kind="ExternalInput").ap())
    outT = nc.dram_tensor("outT", (P, DT, S), F32, kind="ExternalOutput").ap()
    build(nc, *args, outT)
    r = run_bass_kernel_spmd(nc, [arrays], core_ids=[0])
    out = r.results[0]["outT"]
    return out.transpose(1, 0, 2).reshape(1, D, S).transpose(0, 2, 1)
```

```python
from contextlib import ExitStack

import concourse.bass as bass
from concourse import mybir

F32 = mybir.dt.float32
F32R = mybir.dt.float32r
ALU = mybir.AluOpType
ACT = mybir.ActivationFunctionType
AX_X = mybir.AxisListType.X

P = 128
S = 256
D = 2048
DT = D // P
EPS = 1e-6
SCALE = float(P) ** -0.5
HEADS = 8
SSM_HEADS = 16
FF_TILES = 44
FF_GROUPS = FF_TILES // 4
RET_HEADS = 4

RAW = 8
SPLIT = 4
LEAD = 4
B_IN, B_OUT, B_FF = 0, 11, 15
B_IN2 = B_FF + 3 * FF_GROUPS
B_OUT2 = B_IN2 + 14
BLOCKS = B_OUT2 + 4
G_IN, G_OUT, G_FF = 0, 11, 15
G_IN2 = G_FF + 6 * FF_GROUPS
G_OUT2 = G_IN2 + 14

IN_SLOTS, IN2_SLOTS = 8 * 11, 8 * 14
ATT0, ATT1, ATT2, ATT3 = 65, 87, 86, 110
RET0 = 65
Z, Q0, K0, V0, Q1, K1, V1 = 0, 8, 12, 16, 20, 24, 28
ZA2, ZR2, QR2, KR2, VR2, Q02, K02, V02, Q12, K12, V12 = 0, 8, 16, 20, 24, 32, 36, 40, 44, 48, 52
OUT_TILES = [8, 9, 10, 11, 12, 13, 14, 15, 0, 1, 2, 3, 4, 5, 6, 7]
OUT_UNITS = ([(0, k) for k in range(6)] + [(1, k) for k in range(6)] + [(0, 6), (0, 7), (1, 6), (1, 7)]
             + [(2, k) for k in range(8)] + [(3, k) for k in range(8)])


def head_tile(low, high, h):
    return low + h if h < 4 else high + h - 4


COLS = dict(norm1=16, norm2=16, ssm_norm=8, q_norm=1, k_norm=1, gain2=16, final=16, c=16, b_ada=48,
            d_skip=8, ssm_conv=12 * 5, ffn_conv=88 * 4, dt_bias=1, a_log=1, decay=8, eps=1)
AT, _n = {}, 0
for _k, _w in COLS.items():
    AT[_k] = _n
    _n += _w
N_PARAMS = _n
ADA_CHUNK = 1024
ADA_CHUNKS = 3 * D // ADA_CHUNK


def build(nc, xT, weights, w_dt, w_ada, params, const1, const2, outT):
    ctx = ExitStack()
    with ctx:
        at = [(nc.sbuf_base + 127) // 128 * 128]

        def place(name, shape, dtype=F32, offset=None):
            size = 4
            for n in shape[1:]:
                size *= n
            if offset is None:
                offset = at[0]
                at[0] += (size + 31) // 32 * 32
            t = nc.alloc_sbuf_tensor_at(name, shape, dtype, offset=offset)
            return t, offset + (size + 31) // 32 * 32

        def sem(name):
            return ctx.enter_context(nc.semaphore(name))

        X, _ = place("X", [P, DT, S])
        raw, _ = place("raw", [P, RAW, 1024])
        whi, _ = place("whi", [P, SPLIT, 1024], F32R)
        wlo, _ = place("wlo", [P, SPLIT, 1024], F32R)
        gh, _ = place("gh", [P, DT, S], F32R)
        gl, _ = place("gl", [P, DT, S], F32R)
        prm, _ = place("prm", [P, N_PARAMS])
        cst, _ = place("cst", [P, 3 * P + 32])
        rb, _ = place("rb", [P, S])
        small, _ = place("small", [P, 512])
        modT, _ = place("modT", [P, 48])
        ones, ident, tri, ident32 = cst[:, 0:P], cst[:, P:2 * P], cst[:, 2 * P:3 * P], cst[:, 3 * P:]
        ada_at = at[0]
        ada_w, _ = place("ada_w", [P, 2, ADA_CHUNK])
        ada_acc, _ = place("ada_acc", [P, ADA_CHUNKS, ADA_CHUNK])
        area = at[0]
        QKVZ, o = place("QKVZ", [P, 32, S], offset=area)
        U, o = place("U", [P, 12, S + 3], offset=o)
        mask, o = place("mask", [P, 2, S], offset=o)
        conv_acc, _ = place("conv_acc", [P, 4, S], offset=o)
        SB1, o = place("SB1", [P, 2, 2, S], offset=o)
        PTS1, o = place("PTS1", [P, 2, 2, S], offset=o)
        VS1, o = place("VS1", [P, 2, 2, P], offset=o)
        assert o <= nc.sbuf_usable_end, (o, nc.sbuf_usable_end)
        SQX1, _ = place("SQX1", [P, 2, 4, S], offset=area + 1024 * Q0)
        late = area + 1024 * V0
        wdt_f, o = place("wdt_f", [P, DT * 16 + 112], offset=late)
        wdt_h, o = place("wdt_h", [P, DT * 16 + 112], F32R, offset=o)
        wdt_l, o = place("wdt_l", [P, DT * 16 + 112], F32R, offset=o)
        DTW, o = place("DTW", [P, 6, S + 8], offset=o)
        XD, o = place("XD", [P, 2, D // 2], offset=late)
        EM, o = place("EM", [P, 3, 3, P], offset=o)
        CB, o = place("CB", [P, 2, 3, P], offset=o)
        assert o <= area + 1024 * 32
        SQY = [buf[:, :, :, :].rearrange("p a b s -> p (a b) s") for buf in (PTS1, SB1)]
        YB = VS1[:, :, :, :].rearrange("p a b s -> p a (b s)")
        UG, o = place("UG", [P, 4, S + 2], offset=area)
        UV, o = place("UV", [P, 4, S + 2], offset=o)
        CG, o = place("CG", [P, 4, S], offset=o)
        CV, o = place("CV", [P, 4, S], offset=o)
        ah, o = place("ah", [P, 4, S], F32R, offset=o)
        al, o = place("al", [P, 4, S], F32R, offset=o)
        SQX2, o = place("SQX2", [P, 2, 4, S], offset=o)
        ah2, o = place("ah2", [P, 4, S], F32R, offset=o)
        al2, o = place("al2", [P, 4, S], F32R, offset=o)
        TR, o = place("TR", [P, 2, 512], offset=o)
        RQ, o = place("RQ", [P, 192], offset=o)
        TH, _ = place("TH", [P, 8, S], offset=area)
        QB, o = place("QB", [P, 56, S], offset=ada_at)
        c2, o = place("c2", [P, 6, 2, S], offset=o)
        DM, o = place("DM", [P, RET_HEADS, 2, S], offset=o)
        SB2, o = place("SB2", [P, 2, 2, S], offset=o)
        PTS2, o = place("PTS2", [P, 2, 2, S], offset=o)
        VS2, o = place("VS2", [P, 2, 2, P], offset=o)
        assert o <= nc.sbuf_usable_end, (o, nc.sbuf_usable_end)
        E12 = SB2
        SQR = c2[:, 2:4, :, :]
        SQX4, _ = place("SQX4", [P, 2, 4, S], offset=ada_at)
        PS = ctx.enter_context(nc.psum_tensor("PS", [P, 8, 512], F32))

        def col(name, i=0, n=1):
            return prm[:, AT[name] + i:AT[name] + i + n]

        def acc_tiles(par):
            return PS[:, 2 * par:2 * par + 2, :].rearrange("p b (t s) -> p (b t) s", t=2)

        s_prm, s_cst, s_x = sem("s_prm"), sem("s_cst"), [sem(f"s_x{c}") for c in range(4)]
        s_raw = [sem(f"s_raw{j}") for j in range(RAW)]
        s_hi = sem("s_hi")
        s_lo = sem("s_lo")
        s_used = sem("s_used")
        s_evac = sem("s_evac")
        s_gh, s_gl = sem("s_gh"), sem("s_gl")
        s_mask, s_wdt, s_c2, s_out = sem("s_mask"), sem("s_wdt"), sem("s_c2"), sem("s_out")
        s_ready = sem("s_ready")
        s_sq, s_sum, s_ss, s_root, s_rb = (sem("s_sq"), sem("s_sum"), sem("s_ss"), sem("s_root"), sem("s_rb"))
        s_dve = sem("s_dve")
        s_base, s_tap, s_silu = sem("s_base"), sem("s_tap"), sem("s_silu")
        s_fbase, s_ftap, s_fsilu = sem("s_fbase"), sem("s_ftap"), sem("s_fsilu")
        s_prod, s_ah, s_al = sem("s_prod"), sem("s_ah"), sem("s_al")
        s_wdth, s_wdtl, s_dtp = sem("s_wdth"), sem("s_wdtl"), sem("s_dtp")
        s_sp, s_spe, s_spl, s_la = sem("s_sp"), sem("s_spe"), sem("s_spl"), sem("s_la")
        s_dtr, s_dts = sem("s_dtr"), sem("s_dts")
        s_nsq, s_nr, s_nrt, s_qk = sem("s_nsq"), sem("s_nr"), sem("s_nrt"), sem("s_qk")
        s_vt, s_sc, s_pt, s_pv = sem("s_vt"), sem("s_sc"), sem("s_pt"), sem("s_pv")
        s_vs, s_exp, s_pts, s_ahi = sem("s_vs"), sem("s_exp"), sem("s_pts"), sem("s_ahi")
        s_sb, s_nm, s_pn, s_gated = sem("s_sb"), sem("s_nm"), sem("s_pn"), sem("s_gated")
        s_ac, s_at, s_nb, s_cb, s_cbm = sem("s_ac"), sem("s_at"), sem("s_nb"), sem("s_cb"), sem("s_cbm")
        s_xt, s_xd, s_z = sem("s_xt"), sem("s_xd"), sem("s_z")
        s_r, s_e, s_ex, s_m, s_y, s_yo = sem("s_r"), sem("s_e"), sem("s_ex"), sem("s_m"), sem("s_y"), sem("s_yo")
        s_ysq, s_ysum, s_yrt, s_yn = sem("s_ysq"), sem("s_ysum"), sem("s_yrt"), sem("s_yn")
        s_c, s_adaw = sem("s_c"), [sem("s_adaw0"), sem("s_adaw1")]
        s_adam, s_ada, s_pool = sem("s_adam"), sem("s_ada"), sem("s_pool")
        s_tr, s_mod, s_mt = sem("s_tr"), sem("s_mod"), sem("s_mt")
        s_zs, s_de, s_dm, s_rvt, s_rvs = sem("s_zs"), sem("s_de"), sem("s_dm"), sem("s_rvt"), sem("s_rvs")
        s_rsc, s_rm, s_ro, s_or = sem("s_rsc"), sem("s_rm"), sem("s_ro"), sem("s_or")
        s_rsq, s_rsum, s_rrt, s_ry = sem("s_rsq"), sem("s_rsum"), sem("s_rrt"), sem("s_ry")
        s_h, s_fin = sem("s_h"), sem("s_fin")
        s_tile, s_part = sem("s_tile"), sem("s_part")

        block = ctx.enter_context(nc.Block())

        @block.sync
        def _(sp):
            sp.dma_start(prm[:, :], params).then_inc(s_prm, 16)
            for j in range(RAW):
                if j % 2 == 0:
                    c = j // 2
                    sp.dma_start(X[:, 4 * c:4 * c + 4, :], xT[:, 4 * c:4 * c + 4, :]).then_inc(s_x[c], 16)
                sp.dma_start(raw[:, j, :], weights[j, :, :]).then_inc(s_raw[j], 16)
            with sp.Fori(1, BLOCKS) as i:
                for j in range(RAW):
                    sp.wait_ge(s_lo, i * RAW + (j + 1 - RAW))
                    sp.dma_start(raw[:, j, :], weights[bass.ds(i * RAW + j, 1), :, :].rearrange("a p n -> (a p) n")
                                 ).then_inc(s_raw[j], 16)
            for q in range(4):
                sp.wait_ge(s_fin, 4 * q + 4)
                sp.dma_start(outT[:, 4 * q:4 * q + 4, :], X[:, 4 * q:4 * q + 4, :]).then_inc(s_out, 16)
            sp.wait_ge(s_out, 64)

        @block.gpsimd
        def _(pool):
            def load(i, t):
                pool.dma_start(ada_w[:, t % 2, :],
                               w_ada[bass.ds(i * DT + t, 1), :, :].rearrange("a p n -> (a p) n")
                               ).then_inc(s_adaw[t % 2], 16)

            pool.wait_ge(s_c, 1)
            with pool.Fori(0, ADA_CHUNKS) as i:
                acc = ada_acc[:, bass.ds(i, 1), :].rearrange("p a n -> p (a n)")
                load(i, 0)
                for t in range(DT):
                    if t + 1 < DT:
                        load(i, t + 1)
                    w = ada_w[:, t % 2, :]
                    pool.wait_ge(s_adaw[t % 2], i * (16 * DT // 2) + 16 * (t // 2) + 16)
                    pool.sem_inc(s_pool, 1)
                    pool.tensor_scalar(w, w, small[:, 64 + t:65 + t], None, ALU.mult).then_inc(s_adam, 1)
                    pool.wait_ge(s_adam, i * DT + t + 1)
                    pool.sem_inc(s_pool, 1)
                    if t == 0:
                        pool.tensor_copy(acc, w).then_inc(s_ada, 1)
                    else:
                        pool.tensor_tensor(acc, acc, w, ALU.add).then_inc(s_ada, 1)
                    pool.wait_ge(s_ada, i * DT + t + 1)
                    pool.sem_inc(s_pool, 1)

        @block.scalar
        def _(act):
            def split(blk, j):
                blk, j = blk + j // RAW, j % RAW
                act.wait_ge(s_raw[j], blk * 16 + 16)
                act.wait_ge(s_used, blk * RAW + j + 1)
                act.activation(whi[:, j % SPLIT, :], raw[:, j, :], ACT.Copy).then_inc(s_hi, 1)

            def group(blk):
                for j in range(8):
                    split(blk, LEAD + j)

            def squares(k, c, buf):
                if c >= 2:
                    act.wait_ge(s_sum, 2 * k + c - 1)
                if c < 3:
                    act.activation(buf[:, (c > 0) * 1, :, :], X[:, 4 * c:4 * c + 4, :], ACT.Square).then_inc(s_sq, 1)
                    return
                for t in range(4):
                    if k >= 2:
                        act.wait_ge(s_tile, 4 * (k - 2) + t + 1)
                    act.activation(buf[:, 1, t, :], X[:, 12 + t, :], ACT.Square).then_inc(s_sq, 1)

            def root(k, n):
                act.wait_ge(s_ss, k + 1)
                act.activation(rb[:, :], PS[:, 4, 0:S], ACT.Sqrt, bias=col("eps"), scale=1.0 / n).then_inc(s_root, 1)

            def scaled_hi(name, first, end):
                for t in range(first, end):
                    act.activation(gh[:, t, :], X[:, t, :], ACT.Copy, scale=col(name, t)).then_inc(s_gh, 1)

            act.dma_start(cst[:, :], const1[:, 0:3 * P + 32]).then_inc(s_cst, 16)
            act.dma_start(wdt_f[:, :], w_dt).then_inc(s_wdt, 16)
            act.dma_start(mask[:, :, :], const1[:, 3 * P + 32:].rearrange("p (b s) -> p b s", b=2)).then_inc(s_mask, 16)
            act.wait_ge(s_prm, 16)
            act.activation(small[:, 64:80], col("c", 0, 16), ACT.Silu).then_inc(s_c, 1)
            for c in range(4):
                act.wait_ge(s_x[c], 16)
                for t in range(4 * c, 4 * c + 4):
                    act.activation(gh[:, t, :], X[:, t, :], ACT.Copy, scale=col("norm1", t)).then_inc(s_gh, 1)
                split(B_IN, c)

            def ssm_base(g, t):
                act.wait_ge(s_evac, G_IN + g + 3)
                if g:
                    act.wait_ge(s_silu, g)
                w = 5 * (4 * g + t)
                act.activation(conv_acc[:, t, :], U[:, 4 * g + t, 3:3 + S], ACT.Identity,
                               bias=col("ssm_conv", w), scale=col("ssm_conv", w + 4)).then_inc(s_base, 1)

            def ssm_silu(g):
                act.wait_ge(s_tap, 12 * (g + 1))
                act.activation(U[:, 4 * g:4 * g + 4, 3:3 + S], conv_acc[:, :, :], ACT.Silu).then_inc(s_silu, 1)

            def gate_silu(buf, at, evac, signal):
                act.wait_ge(s_evac, evac)
                act.activation(buf[:, at:at + 4, :], buf[:, at:at + 4, :], ACT.Silu).then_inc(signal, 1)

            def head_squares(h):
                if h == 0:
                    act.wait_ge(s_ysum, 2)
                if h >= 2:
                    act.wait_ge(s_nr, h - 1)
                act.wait_ge(s_evac, (G_IN + 7 if h < 4 else G_IN + 10) + 2)
                q = head_tile(Q0, Q1, h)
                act.activation(PTS1[:, h % 2, :, :], QKVZ[:, q:q + 5:4, :], ACT.Square).then_inc(s_nsq, 1)

            def head_root(h):
                act.wait_ge(s_nr, h + 1)
                if h >= 2:
                    act.wait_ge(s_qk, 2 * h - 2)
                act.activation(SB1[:, h % 2, :, :], PS[:, 6 + h % 2, :].rearrange("p (c d) -> p c d", c=2), ACT.Sqrt,
                               bias=col("eps"), scale=1.0 / P).then_inc(s_nrt, 1)

            def attention(step, h, layer):
                H = layer * HEADS + h
                SB, PTS, VS = (SB2, PTS2, VS2) if layer else (SB1, PTS1, VS1)
                if step == 3:
                    act.wait_ge(s_vt, H + 1)
                    if H >= 2:
                        act.wait_ge(s_pv, H - 1)
                    act.activation(VS[:, h % 2, :, :], PS[:, 7, 0:S].rearrange("p (c d) -> p c d", c=2),
                                   ACT.Copy).then_inc(s_vs, 1)
                if step == 1:
                    act.wait_ge(s_nm, H + 1)
                    for b in range(2):
                        k = 2 * (h % 2) + b
                        act.activation(SB[:, h % 2, b, :], SB[:, h % 2, b, :], ACT.Exp, bias=small[:, k:k + 1],
                                       accum_out=small[:, 4 + k:5 + k]).then_inc(s_exp, 1)
                if step == 3:
                    act.wait_ge(s_pt, H + 1)
                    if H >= 2:
                        act.wait_ge(s_pv, H - 1)
                    act.activation(PTS[:, h % 2, :, :], PS[:, 5, :].rearrange("p (c d) -> p c d", c=2),
                                   ACT.Copy).then_inc(s_pts, 1)
                if step == 5 and layer == 0:
                    act.wait_ge(s_pv, H + 1)
                    if h < 4:
                        act.activation(QKVZ[:, Q0 + h, :], PS[:, 6, 0:S], ACT.Copy).then_inc(s_ahi, 1)
                    else:
                        act.activation(gh[:, 8 + h, :], PS[:, 6, 0:S], ACT.Copy).then_inc(s_ahi, 1)
                if step == 5 and layer == 1 and h >= 4:
                    act.wait_ge(s_gated, h + 1)
                    act.activation(gh[:, 8 + h, :], QB[:, ZA2 + h, :], ACT.Copy).then_inc(s_ahi, 1)

            def attention_slot(n, b, h0, layer):
                for h in range(h0, h0 + 4):
                    step = n - (b + 2 * (h - h0))
                    if 0 <= step < 6:
                        attention(step, h, layer)

            def converted(k, buf, a, b):
                src = a + 2 * k if k < 4 else b + 2 * (k - 4)
                act.activation(gh[:, 2 * k:2 * k + 2, :], buf[:, src:src + 2, :], ACT.Copy).then_inc(s_gh, 1)

            def slot1(n):
                if n < 4:
                    squares(0, n, SQX1)
                if n == 4:
                    act.wait_ge(s_wdt, 16)
                    act.activation(wdt_h[:, :], wdt_f[:, :], ACT.Copy).then_inc(s_wdth, 1)
                if n == 5:
                    root(0, D)
                g, j = n // 8 - 1, n % 8
                if 0 <= g < 3:
                    if j < 4:
                        ssm_base(g, j)
                    if j == 6:
                        ssm_silu(g)
                if n == 10:
                    act.wait_ge(s_sp, 1)
                    act.activation(DTW[:, 2, :], DTW[:, 1, :], ACT.Exp, scale=-1.0).then_inc(s_spe, 1)
                    act.activation(small[:, 168:169], col("a_log"), ACT.Exp).then_inc(s_spe, 1)
                if n == 11:
                    act.wait_ge(s_sp, 2)
                    act.activation(DTW[:, 4, :], DTW[:, 3, :], ACT.Ln).then_inc(s_spl, 1)
                if n == 19:
                    act.wait_ge(s_ac, 1)
                    act.activation(small[0:16, 256:512], PS[0:16, 7, S:2 * S], ACT.Copy).then_inc(s_at, 1)
                if n == 33:
                    gate_silu(QKVZ, Z, G_IN + 4 + 2, s_z)
                if n == 41:
                    gate_silu(QKVZ, Z + 4, G_IN + 5 + 2, s_z)
                if 35 <= n < 35 + SSM_HEADS:
                    h = n - 35
                    act.wait_ge(s_e, 3 * h + 3)
                    act.activation(EM[:, h % 3, :, :], EM[:, h % 3, :, :], ACT.Exp).then_inc(s_ex, 1)
                for g in range(2):
                    if n == 53 + g:
                        act.wait_ge(s_yo, 16)
                        act.activation(SQY[g], QKVZ[:, Z + 4 * g:Z + 4 * g + 4, :], ACT.Square).then_inc(s_ysq, 1)
                    if n == 55 + g:
                        act.wait_ge(s_ysum, g + 1)
                        act.activation(YB[:, g, :], PS[:, 6 + g, 0:S], ACT.Sqrt, bias=col("eps"), scale=1.0 / 512
                                       ).then_inc(s_yrt, 1)
                for b, h0 in ((58, 0), (80, 4)):
                    h, odd = divmod(n - b, 2)
                    if not odd and 0 <= h < 4:
                        head_squares(h0 + h)
                    if not odd and 1 <= h < 5:
                        head_root(h0 + h - 1)
                if 0 <= n - (IN_SLOTS - 8) < 6:
                    act.wait_ge(s_yn, 8)
                    converted(n - (IN_SLOTS - 8), QKVZ, Z, Q0)
                attention_slot(n, ATT0, 0, 0)
                attention_slot(n, ATT1, 4, 0)

            for n in range(IN_SLOTS):
                split(B_IN, LEAD + n)
                slot1(n)
            for s in range(32):
                split(B_OUT, LEAD + s)
                slot1(IN_SLOTS + s)
                if s in (13, 15, 23, 31):
                    c = (13, 15, 23, 31).index(s)
                    act.wait_ge(s_evac, G_OUT + c + 3)
                    squares(1, c, SQX2)
                if 24 <= s < 30:
                    scaled_hi("norm2", 2 * (s - 24), 2 * (s - 24) + 2)
            scaled_hi("norm2", 12, DT)

            def ffn_base(i, val):
                src, dst = (UV, CV) if val else (UG, CG)
                for t in range(4):
                    k = (i * 4 + t + (FF_TILES if val else 0)) * 4 + AT["ffn_conv"]
                    act.activation(dst[:, t, :], src[:, t, 2:2 + S], ACT.Identity, bias=prm[:, bass.ds(k, 1)],
                                   scale=prm[:, bass.ds(k + 3, 1)]).then_inc(s_fbase, 1)

            def ffn_silu(i):
                act.wait_ge(s_ftap, i * 16 + 8)
                act.activation(CG[:, :, :], CG[:, :, :], ACT.Silu).then_inc(s_fsilu, 1)

            def ffn_hi(i, hi=ah):
                act.wait_ge(s_prod, i + 1)
                act.activation(hi[:, :, :], CG[:, :, :], ACT.Copy).then_inc(s_ah, 1)

            group(B_FF)
            root(1, D)
            split(B_FF + 1, LEAD)
            act.wait_ge(s_evac, G_FF + 1 + 2)
            ffn_base(0, False)
            for j in range(1, 8):
                split(B_FF + 1, LEAD + j)
            act.wait_ge(s_evac, G_FF + 2 + 2)
            ffn_base(0, True)
            def ffn(i):
                blk = i * 3 + (B_FF - 1)
                grp = i * 6 + (G_FF - 4)
                split(blk, LEAD)
                ffn_silu(i - 1)
                for j in range(1, 4):
                    split(blk, LEAD + j)
                ffn_hi(i - 1)
                for j in range(4, 8):
                    split(blk, LEAD + j)
                split(blk + 1, LEAD)
                act.wait_ge(s_evac, grp + 3)
                ffn_base(i, False)
                for j in range(1, 8):
                    split(blk + 1, LEAD + j)
                split(blk + 2, LEAD)
                act.wait_ge(s_evac, grp + 4)
                ffn_base(i, True)
                for j in range(1, 8):
                    split(blk + 2, LEAD + j)
                    if i is last and j == 4:
                        ffn_silu(i)
                    if i is last and j == 7:
                        ffn_hi(i, ah2)

            last = FF_GROUPS - 1
            with act.Fori(1, last) as i:
                ffn(i)
            ffn(last)
            for d in range(4):
                split(B_IN2 - 1, LEAD + 2 * d)
                split(B_IN2 - 1, LEAD + 2 * d + 1)
                if d < 3:
                    act.wait_ge(s_evac, G_IN2 - 4 + d + 3)
                squares(2, d, SQX2)
            root(2, D)
            for t in range(DT):
                act.wait_ge(s_h, t + 1)
                act.activation(gh[:, t, :], TH[:, t % 8, :], ACT.Identity, bias=modT[:, t:t + 1]).then_inc(s_gh, 1)
            act.dma_start(c2[:, :, :, :], const2).then_inc(s_c2, 16)
            def slot2(n):
                if n in (16, 17):
                    gate_silu(QB, ZA2 + 4 * (n - 16), G_IN2 + 2 + 2, s_zs)
                if n in (32, 33):
                    gate_silu(QB, ZR2 + 4 * (n - 32), G_IN2 + 4 + 2, s_zs)
                if n in (36, 38, 40, 42):
                    r = (n - 36) // 2
                    if r == 0:
                        act.wait_ge(s_c2, 16)
                    else:
                        act.wait_ge(s_dm, r)
                    for k in range(2):
                        act.activation(E12[:, k, :, :], c2[:, 2 + k, :, :], ACT.Exp,
                                       scale=small[:, 248 + 4 * k + r:249 + 4 * k + r]).then_inc(s_de, 1)
                for r in range(RET_HEADS):
                    step = n - (RET0 + 2 * r)
                    if step == 0:
                        act.wait_ge(s_rvt, r + 1)
                        if r >= 2:
                            act.wait_ge(s_ro, r - 1)
                        act.activation(PTS2[:, r % 2, :, :], PS[:, 4, :].rearrange("p (c d) -> p c d", c=2),
                                       ACT.Copy).then_inc(s_rvs, 1)
                    if step == 3:
                        act.wait_ge(s_or, r + 1)
                        if r >= 2:
                            act.wait_ge(s_rsum, r - 1)
                        act.activation(SQR[:, r % 2, :, :], QB[:, VR2 + 2 * r:VR2 + 2 * r + 2, :], ACT.Square
                                       ).then_inc(s_rsq, 1)
                    if step == 5:
                        act.wait_ge(s_rsum, r + 1)
                        act.activation(VS2[:, r % 2, :, :], PS[:, 7, 0:S].rearrange("p (c d) -> p c d", c=2), ACT.Sqrt,
                                       bias=col("eps"), scale=1.0 / S).then_inc(s_rrt, 1)
                if 0 <= n - (IN2_SLOTS - 8) < 6:
                    act.wait_ge(s_ry, 2 * RET_HEADS)
                    act.wait_ge(s_gated, 4)
                    converted(n - (IN2_SLOTS - 8), QB, ZR2, ZA2)
                attention_slot(n, ATT2, 0, 1)
                attention_slot(n, ATT3, 4, 1)

            for n in range(IN2_SLOTS):
                split(B_IN2, LEAD + n)
                if n % 8 == 7:
                    g = n // 8
                    act.wait_ge(s_used, 8 * B_IN2 + n + 1 + SPLIT)
                    act.activation(QB[:, 4 * g:4 * g + 4, :], acc_tiles((G_IN2 + g) % 2), ACT.Copy).then_inc(s_evac, 1)
                slot2(n)
            for s in range(32):
                if s < 28:
                    split(B_OUT2, LEAD + s)
                slot2(IN2_SLOTS + s)
                if s in (13, 15, 23, 31):
                    c = (13, 15, 23, 31).index(s)
                    if c < 3:
                        act.wait_ge(s_evac, G_OUT2 + c + 3)
                    squares(3, c, SQX4)
            root(3, D)

        @block.vector
        def _(dve):
            links = [0]

            def link(ins):
                links[0] += 1
                ins.then_inc(s_dve, 1)
                dve.wait_ge(s_dve, links[0])

            def split(blk, j):
                blk, j = blk + j // RAW, j % RAW
                dve.wait_ge(s_hi, blk * RAW + j + 1)
                dve.tensor_tensor(wlo[:, j % SPLIT, :], raw[:, j, :], whi[:, j % SPLIT, :].bitcast(F32),
                                  ALU.subtract).then_inc(s_lo, 1)

            def group(blk):
                for j in range(8):
                    split(blk, LEAD + j)

            def finished(last, grp):
                dve.wait_ge(s_used, last + 1 + SPLIT)
                dve.wait_ge(s_evac, grp + 2)

            def add_to_x(last, grp, par, first):
                finished(last, grp)
                x = X[:, first:first + 4, :]
                dve.tensor_tensor(x, acc_tiles(par), x, ALU.add).then_inc(s_evac, 1)

            def scaled_lo(base, name, first, end):
                for t in range(first, end):
                    dve.wait_ge(s_gh, base + t + 1)
                    dve.scalar_tensor_tensor(gl[:, t, :], X[:, t, :], col(name, t), gh[:, t, :].bitcast(F32),
                                             ALU.mult, ALU.subtract).then_inc(s_gl, 1)

            def sum_chunk(k, c, buf):
                dve.wait_ge(s_sq, 7 * k + c + 1)
                if c > 1:
                    dve.wait_ge(s_sum, 2 * k + c - 1)
                dve.tensor_tensor(buf[:, 0, :, :], buf[:, 0, :, :], buf[:, 1, :, :], ALU.add).then_inc(s_sum, 1)

            def inverse_root(k):
                dve.wait_ge(s_root, k + 1)
                dve.reciprocal(rb[:, :], rb[:, :]).then_inc(s_rb, 1)

            dve.sem_inc(s_evac, 2)
            dve.wait_ge(s_prm, 16)
            for c in range(4):
                for t in range(4 * c, 4 * c + 4):
                    dve.wait_ge(s_gh, t + 1)
                    dve.scalar_tensor_tensor(gl[:, t, :], X[:, t, :], col("norm1", t), gh[:, t, :].bitcast(F32),
                                             ALU.mult, ALU.subtract).then_inc(s_gl, 1)
                split(B_IN, c)
            dve.memset(U[:, :, 0:3], 0.0).then_inc(s_ready, 1)

            def ssm_evac(g):
                finished(8 * (B_IN + g) + 7, G_IN + g)
                dve.wait_ge(s_rb, 1)
                dve.tensor_tensor(U[:, 4 * g:4 * g + 4, 3:3 + S], acc_tiles((G_IN + g) % 2),
                                  rb[:, :].unsqueeze(1).to_broadcast([P, 4, S]), ALU.mult).then_inc(s_evac, 1)

            def ssm_taps(g, t):
                w = 5 * (4 * g + t)
                dve.wait_ge(s_base, 4 * g + t + 1)
                for k in range(3):
                    if k:
                        dve.wait_ge(s_tap, 12 * g + 3 * t + k)
                    dve.scalar_tensor_tensor(conv_acc[:, t, :], U[:, 4 * g + t, 2 - k:2 - k + S],
                                             col("ssm_conv", w + 3 - k), conv_acc[:, t, :], ALU.mult, ALU.add
                                             ).then_inc(s_tap, 1)

            def land(g):
                finished(8 * (B_IN + g) + 7, G_IN + g)
                dve.tensor_tensor(QKVZ[:, 4 * (g - 3):4 * (g - 3) + 4, :], acc_tiles((G_IN + g) % 2),
                                  rb[:, :].unsqueeze(1).to_broadcast([P, 4, S]), ALU.mult).then_inc(s_evac, 1)

            W = [DTW[:, k, :] for k in range(6)]

            def dt_steps(n):
                if n == 10:
                    dve.wait_ge(s_dtp, 1)
                    link(dve.tensor_tensor(W[0][:, 0:S], PS[:, 5, 0:S], rb[:, :], ALU.mult))
                    dve.tensor_scalar(W[0][:, 0:S], W[0][:, 0:S], col("dt_bias"), None, ALU.add)
                    link(dve.tensor_copy(W[0][:, S:], col("decay", 0, 8)))
                    dve.scalar_tensor_tensor(W[1], W[0], -1.0, W[0], ALU.mult, ALU.max).then_inc(s_sp, 1)
                if n == 11:
                    dve.wait_ge(s_spe, 1)
                    dve.tensor_scalar(W[3], W[2], 1.0, None, ALU.add).then_inc(s_sp, 1)
                    dve.wait_ge(s_sp, 2)
                    link(dve.tensor_scalar(W[1], W[3], 1.0, None, ALU.is_equal))
                if n == 12:
                    link(dve.scalar_tensor_tensor(W[5], W[3], -1.0, W[1], ALU.add, ALU.add))
                    link(dve.reciprocal(W[5], W[5]))
                if n == 13:
                    dve.wait_ge(s_spl, 1)
                    link(dve.tensor_tensor(W[4], W[4], W[1], ALU.add))
                    link(dve.tensor_tensor(W[4], W[4], W[5], ALU.mult))
                if n == 14:
                    link(dve.tensor_tensor(W[4], W[4], W[2], ALU.mult))
                    link(dve.scalar_tensor_tensor(small[:, 248:256], W[0][:, S:], 0.0, W[4][:, S:], ALU.min, ALU.subtract))
                    link(dve.scalar_tensor_tensor(W[1][:, 0:S], W[0][:, 0:S], 0.0, W[4][:, 0:S], ALU.max, ALU.add))
                if n == 15:
                    dve.wait_ge(s_spe, 2)
                    dve.tensor_scalar(W[3][:, 0:S], W[1][:, 0:S], small[:, 168:169], -1.0, ALU.mult, ALU.mult).then_inc(s_la, 1)
                if n == 17:
                    dve.wait_ge(s_dtr, 1)
                    dve.tensor_copy(small[:, 16:48], PS[:, 5, 0:32]).then_inc(s_dts, 1)
                    dve.tensor_copy(small[:, 88:120], PS[:, 5, 32:64]).then_inc(s_dts, 1)

            NB = small[:, 176:224].rearrange("p (k h) -> p k h", k=3)

            def bias_steps():
                dve.wait_ge(s_ac, 1)
                dve.wait_ge(s_at, 1)
                dve.tensor_scalar(NB[:, 0, :], PS[:, 7, 0:16], -1.0, None, ALU.mult)
                link(dve.tensor_scalar(NB[:, 2, :], PS[:, 7, 16:32], -1.0, None, ALU.mult))
                dve.tensor_tensor(NB[:, 1, :], PS[:, 7, 32:48], NB[:, 0, :], ALU.add).then_inc(s_nb, 1)

            def spread_x(j):
                dve.wait_ge(s_xt, j + 1)
                if j == 0:
                    dve.wait_ge(s_dts, 2)
                for c in range(2):
                    dve.tensor_tensor(XD[:, c, P * j:P * j + P].rearrange("p (h d) -> p h d", h=2),
                                      PS[:, 4 + j % 2, P * c:P * c + P].rearrange("p (h d) -> p h d", h=2),
                                      small[:, 16 + 16 * c + 2 * j:18 + 16 * c + 2 * j].unsqueeze(2).to_broadcast([P, 2, 64]),
                                      ALU.mult).then_inc(s_xd, 1)

            def masked(g):
                dve.wait_ge(s_cb, g + 1)
                cb = PS[:, 6 + g, 0:3 * P].rearrange("p (k l) -> p k l", k=3)
                dve.tensor_tensor(CB[:, g, 0:3:2, :], cb[:, 0:3:2, :], tri.unsqueeze(1).to_broadcast([P, 2, P]), ALU.mult
                                  ).then_inc(s_cbm, 1)
                dve.tensor_copy(CB[:, g, 1, :], cb[:, 1, :]).then_inc(s_cbm, 1)

            def decay(h):
                dve.wait_ge(s_r, h + 1)
                if h == 0:
                    dve.wait_ge(s_nb, 1)
                if h >= 3:
                    dve.wait_ge(s_y, h - 2)
                for k in range(3):
                    lo = P if k else 0
                    dve.tensor_scalar(EM[:, h % 3, k, :], PS[:, 4 + h % 2, lo:lo + P], NB[:, k, h:h + 1], 0.0,
                                      ALU.add, ALU.min).then_inc(s_e, 1)

            def weigh(h):
                dve.wait_ge(s_ex, h + 1)
                if h == 0:
                    dve.wait_ge(s_cbm, 4)
                dve.tensor_tensor(EM[:, h % 3, :, :], EM[:, h % 3, :, :], CB[:, h // 8, :, :], ALU.mult).then_inc(s_m, 1)

            def ssm_out(j):
                dve.wait_ge(s_y, 2 * j + 2)
                dve.wait_ge(s_z, 1 + j // 4)
                if j >= 2:
                    dve.wait_ge(s_yo, 2 * j - 2)
                dve.scalar_tensor_tensor(YB[:, j % 2, :], U[:, j, 3:3 + S], col("d_skip", j), PS[:, 6 + j % 2, 0:S],
                                         ALU.mult, ALU.add).then_inc(s_yo, 1)
                dve.wait_ge(s_yo, 2 * j + 1)
                dve.tensor_tensor(QKVZ[:, Z + j, :], YB[:, j % 2, :], QKVZ[:, Z + j, :], ALU.mult).then_inc(s_yo, 1)

            def ssm_norm(g):
                dve.wait_ge(s_yrt, g + 1)
                link(dve.reciprocal(YB[:, g, :], YB[:, g, :]))
                for t in range(4):
                    y = QKVZ[:, Z + 4 * g + t, :]
                    dve.scalar_tensor_tensor(y, y, col("ssm_norm", 4 * g + t), YB[:, g, :], ALU.mult, ALU.mult
                                             ).then_inc(s_yn, 1)

            def head_norm(h):
                dve.wait_ge(s_nrt, h + 1)
                link(dve.reciprocal(SB1[:, h % 2, :, :], SB1[:, h % 2, :, :]))
                for k in range(2):
                    t = QKVZ[:, head_tile(Q0, Q1, h) + 4 * k, :]
                    dve.scalar_tensor_tensor(t, t, col("k_norm" if k else "q_norm"), SB1[:, h % 2, k, :],
                                             ALU.mult, ALU.mult).then_inc(s_qk, 1)

            def attention(step, h, layer):
                H = layer * HEADS + h
                SB = SB2 if layer else SB1
                if step == 0:
                    if layer:
                        if h >= 2:
                            dve.wait_ge(s_pt, H - 1)
                        link(dve.scalar_tensor_tensor(SB[:, h % 2, :, :], c2[:, 0, :, :], -2.0 ** -(h + 1),
                                                      c2[:, 1, :, :], ALU.mult, ALU.add))
                    dve.wait_ge(s_sc, H + 1)
                    if not layer and h % 4 < 2:
                        dve.wait_ge(s_qk, 2 * h + 6)
                    if H >= 2:
                        dve.wait_ge(s_pt, H - 1)
                    dve.scalar_tensor_tensor(SB[:, h % 2, :, :], PS[:, 4, :].rearrange("p (c d) -> p c d", c=2),
                                             SCALE, SB[:, h % 2, :, :] if layer else mask[:, :, :],
                                             ALU.mult, ALU.add).then_inc(s_sb, 1)
                    dve.wait_ge(s_sb, H + 1)
                    k = 2 * (h % 2)
                    dve.tensor_reduce(small[:, k:k + 2], SB[:, h % 2, :, :], AX_X, ALU.max, negate=True).then_inc(s_nm, 1)
                if step == 1:
                    k = 2 * (h % 2)
                    dve.wait_ge(s_exp, 2 * H + 2)
                    link(dve.reciprocal(small[:, 8 + k:10 + k], small[:, 4 + k:6 + k]))
                    for b in range(2):
                        dve.tensor_scalar(SB[:, h % 2, b, :], SB[:, h % 2, b, :], small[:, 8 + k + b:9 + k + b], None,
                                          ALU.mult).then_inc(s_pn, 1)
                if step == 5 and layer:
                    dve.wait_ge(s_pv, H + 1)
                    z = QB[:, ZA2 + h, :]
                    dve.tensor_tensor(z, PS[:, 6, 0:S], z, ALU.mult).then_inc(s_gated, 1)
                    if h >= 4:
                        dve.wait_ge(s_gated, h + 1)
                        dve.wait_ge(s_ahi, H - 3)
                        dve.tensor_tensor(gl[:, 8 + h, :], z, gh[:, 8 + h, :].bitcast(F32), ALU.subtract).then_inc(s_gl, 1)
                if step == 5 and not layer and h >= 4:
                    dve.wait_ge(s_ahi, h + 1)
                    dve.tensor_tensor(gl[:, 8 + h, :], PS[:, 6, 0:S], gh[:, 8 + h, :].bitcast(F32),
                                      ALU.subtract).then_inc(s_gl, 1)

            def attention_slot(n, b, h0, layer):
                for h in range(h0, h0 + 4):
                    step = n - (b + 2 * (h - h0))
                    if 0 <= step < 6:
                        attention(step, h, layer)

            def converted(k, before, buf, a, b):
                src = a + 2 * k if k < 4 else b + 2 * (k - 4)
                dve.wait_ge(s_gh, before + k + 1)
                dve.tensor_tensor(gl[:, 2 * k:2 * k + 2, :], buf[:, src:src + 2, :], gh[:, 2 * k:2 * k + 2, :].bitcast(F32),
                                  ALU.subtract).then_inc(s_gl, 1)

            def slot1(n):
                if 1 <= n < 3:
                    sum_chunk(0, n, SQX1)
                if n == 5:
                    dve.wait_ge(s_wdth, 1)
                    dve.tensor_tensor(wdt_l[:, :], wdt_f[:, :], wdt_h[:, :].bitcast(F32), ALU.subtract).then_inc(s_wdtl, 1)
                if n == 6:
                    inverse_root(0)
                    dve.wait_ge(s_rb, 1)
                    dve.wait_ge(s_ready, 1)
                g, j = n // 8 - 1, n % 8
                if 0 <= g < 3 and 1 <= j < 5:
                    ssm_taps(g, j - 1)
                dt_steps(n)
                if n == 20:
                    bias_steps()
                if 24 <= n < 32:
                    spread_x(n - 24)
                if n in (32, 33):
                    masked(n - 32)
                if 34 <= n < 34 + SSM_HEADS:
                    decay(n - 34)
                if 35 <= n < 35 + SSM_HEADS:
                    weigh(n - 35)
                if 38 <= n < 54 and n % 2 == 0:
                    ssm_out((n - 38) // 2)
                if n in (56, 57):
                    ssm_norm(n - 56)
                if n in (60, 62, 64, 66):
                    head_norm((n - 60) // 2)
                if n in (82, 84, 86, 88):
                    head_norm((n - 82) // 2 + 4)
                if 0 <= n - (IN_SLOTS - 8) < 6:
                    dve.wait_ge(s_ahi, 4)
                    converted(n - (IN_SLOTS - 8), DT, QKVZ, Z, Q0)
                attention_slot(n, ATT0, 0, 0)
                attention_slot(n, ATT1, 4, 0)

            for n in range(IN_SLOTS):
                split(B_IN, LEAD + n)
                if n == 64:
                    dve.wait_ge(s_mask, 16)
                if n % 8 == 7:
                    if n < 24:
                        ssm_evac(n // 8)
                    else:
                        land(n // 8)
                slot1(n)
            for s in range(32):
                split(B_OUT, LEAD + s)
                slot1(IN_SLOTS + s)
                if s in (13, 15, 23, 31):
                    c = (13, 15, 23, 31).index(s)
                    add_to_x(8 * B_OUT + s, G_OUT + c, (G_OUT + c) % 2, 4 * c)
                    if 0 < c < 3:
                        sum_chunk(1, c, SQX2)
                if 24 <= s < 30:
                    scaled_lo(DT + 6, "norm2", 2 * (s - 24), 2 * (s - 24) + 2)
            scaled_lo(DT + 6, "norm2", 12, DT)
            dve.memset(UG[:, :, 0:2], 0.0).then_inc(s_ready, 1)
            dve.memset(UV[:, :, 0:2], 0.0).then_inc(s_ready, 1)

            def ffn_evac(last, grp, par, dst):
                finished(last, grp)
                dve.tensor_tensor(dst[:, :, 2:2 + S], acc_tiles(par), rb[:, :].unsqueeze(1).to_broadcast([P, 4, S]),
                                  ALU.mult).then_inc(s_evac, 1)

            def ffn_taps(i, val, t):
                src, dst = (UV, CV) if val else (UG, CG)
                k = (i * 4 + t + (FF_TILES if val else 0)) * 4 + AT["ffn_conv"]
                n = 4 if val else 0
                dve.wait_ge(s_fbase, i * 8 + (n + t + 1))
                dve.scalar_tensor_tensor(dst[:, t, :], src[:, t, 1:1 + S], prm[:, bass.ds(k + 2, 1)], dst[:, t, :],
                                         ALU.mult, ALU.add).then_inc(s_ftap, 1)
                dve.wait_ge(s_ftap, i * 16 + (2 * (n + t) + 1))
                dve.scalar_tensor_tensor(dst[:, t, :], src[:, t, 0:S], prm[:, bass.ds(k + 1, 1)], dst[:, t, :],
                                         ALU.mult, ALU.add).then_inc(s_ftap, 1)

            def ffn_product(i):
                dve.wait_ge(s_fsilu, i + 1)
                dve.wait_ge(s_ftap, i * 16 + 16)
                dve.tensor_tensor(CG[:, :, :], CG[:, :, :], CV[:, :, :], ALU.mult).then_inc(s_prod, 1)

            def ffn_lo(i, hi=ah, lo=al):
                dve.wait_ge(s_ah, i + 1)
                dve.tensor_tensor(lo[:, :, :], CG[:, :, :], hi[:, :, :].bitcast(F32), ALU.subtract).then_inc(s_al, 1)

            group(B_FF)
            inverse_root(1)
            dve.wait_ge(s_rb, 2)
            dve.wait_ge(s_ready, 3)
            ffn_evac(8 * B_FF + 7, G_FF, G_FF % 2, UG)
            split(B_FF + 1, LEAD)
            for j in range(1, 8):
                split(B_FF + 1, LEAD + j)
                if 2 <= j < 6:
                    ffn_taps(0, False, j - 2)
            ffn_evac(8 * B_FF + 15, G_FF + 1, (G_FF + 1) % 2, UV)
            for t in range(4):
                ffn_taps(0, True, t)
            last = FF_GROUPS - 1

            def ada_sums(c):
                if c >= 2:
                    dve.wait_ge(s_tr, 2 * c - 2)
                dve.transpose(TR[:, c % 2, :], ada_acc[:, c // 2, 512 * (c % 2):512 * (c % 2) + 512]).then_inc(s_tr, 1)
                dve.wait_ge(s_tr, 2 * c + 1)
                dve.tensor_reduce(RQ[:, 16 * c:16 * c + 16], TR[:, c % 2, :].rearrange("p (b i) -> p b i", i=32), AX_X,
                                  ALU.add).then_inc(s_tr, 1)

            def ffn(i, chunk=None):
                blk = i * 3 + (B_FF - 1)
                unit = i * 24 + 8 * (B_FF - 1)
                grp = i * 6 + (G_FF - 4)
                for j in range(8):
                    split(blk, LEAD + j)
                    if j == 1:
                        ffn_product(i - 1)
                    if j == 5:
                        ffn_lo(i - 1)
                    if chunk is not None and j not in (1, 5):
                        ada_sums(chunk + j - (j > 1) - (j > 5))
                ffn_evac(unit + 7, grp, G_FF % 2, UG)
                for j in range(8):
                    split(blk + 1, LEAD + j)
                    if 2 <= j < 6:
                        ffn_taps(i, False, j - 2)
                ffn_evac(unit + 15, grp + 1, (G_FF + 1) % 2, UV)
                for j in range(8):
                    split(blk + 2, LEAD + j)
                    if i is last and j == 7:
                        ffn_lo(i, ah2, al2)
                    if j % 2:
                        add_to_x(unit + (16 + j), grp + (2 + j // 2), (G_FF + j // 2) % 2, 4 * (j // 2))
                    if 2 <= j < 6:
                        ffn_taps(i, True, j - 2)
                    if i is last and j == 6:
                        ffn_product(i)

            with dve.Fori(1, FF_GROUPS - 2) as i:
                ffn(i)
            dve.wait_ge(s_ada, ADA_CHUNKS * DT)
            ffn(FF_GROUPS - 2, 0)
            ffn(last, 6)
            dve.wait_ge(s_mod, 1)
            link(dve.tensor_tensor(modT[:, :], PS[:, 5, 0:48], col("b_ada", 0, 48), ALU.add))
            dve.scalar_tensor_tensor(modT[:, 16:32], modT[:, 16:32], 1.0, col("gain2", 0, 16), ALU.add, ALU.mult
                                     ).then_inc(s_mt, 1)
            for d in range(4):
                split(B_IN2 - 1, LEAD + 2 * d)
                split(B_IN2 - 1, LEAD + 2 * d + 1)
                if d < 3:
                    add_to_x(8 * (B_IN2 - 1) + 2 * d + 1, G_IN2 - 4 + d, (G_IN2 - 4 + d) % 2, 4 * d)
                if 0 < d < 3:
                    sum_chunk(2, d, SQX2)
            finished(8 * B_IN2 - 1, G_IN2 - 1)
            for t in range(4):
                dve.tensor_tensor(X[:, 12 + t, :], acc_tiles((G_IN2 - 1) % 2)[:, t, :], X[:, 12 + t, :], ALU.add
                                  ).then_inc(s_tile, 1)
            dve.wait_ge(s_tile, 4)
            dve.sem_inc(s_evac, 1)
            inverse_root(2)
            dve.wait_ge(s_mt, 1)
            dve.wait_ge(s_rb, 3)
            for t in range(DT + 1):
                if t < DT:
                    if t >= 8:
                        dve.wait_ge(s_gl, 2 * DT + 10 + t - 7)
                    dve.scalar_tensor_tensor(TH[:, t % 8, :], X[:, t, :], modT[:, 16 + t:17 + t], rb[:, :],
                                             ALU.mult, ALU.mult).then_inc(s_h, 1)
                if t:
                    k = t - 1
                    dve.wait_ge(s_gh, 2 * DT + 6 + k + 1)
                    dve.scalar_tensor_tensor(gl[:, k, :], TH[:, k % 8, :], modT[:, k:k + 1], gh[:, k, :].bitcast(F32),
                                             ALU.add, ALU.subtract).then_inc(s_gl, 1)
            def decays(r):
                dve.wait_ge(s_de, 2 * r + 2)
                if r == 0:
                    dve.wait_ge(s_c2, 16)
                for k in range(2):
                    dve.tensor_tensor(E12[:, k, :, :], E12[:, k, :, :], c2[:, 4 + k, :, :], ALU.mult).then_inc(s_dve, 1)
                links[0] += 2
                dve.wait_ge(s_dve, links[0])
                dve.tensor_tensor(DM[:, r, :, :], E12[:, 0, :, :], E12[:, 1, :, :], ALU.add).then_inc(s_dm, 1)

            def decayed(r):
                dve.wait_ge(s_rsc, r + 1)
                if r >= 2:
                    dve.wait_ge(s_ro, r - 1)
                if r == 0:
                    dve.wait_ge(s_dm, RET_HEADS)
                dve.scalar_tensor_tensor(SB2[:, r % 2, :, :], PS[:, 5, :].rearrange("p (c d) -> p c d", c=2),
                                         SCALE, DM[:, r, :, :], ALU.mult, ALU.mult).then_inc(s_rm, 1)

            def retained(r):
                dve.wait_ge(s_ro, r + 1)
                dve.tensor_copy(QB[:, VR2 + 2 * r:VR2 + 2 * r + 2, :], PS[:, 6, :].rearrange("p (c d) -> p c d", c=2)
                                ).then_inc(s_or, 1)

            def gated(r):
                dve.wait_ge(s_rrt, r + 1)
                link(dve.reciprocal(VS2[:, r % 2, :, :], VS2[:, r % 2, :, :]))
                inv = VS2[:, r % 2, :, :].rearrange("p c d -> p (c d)").unsqueeze(1).to_broadcast([P, 2, S])
                z = QB[:, ZR2 + 2 * r:ZR2 + 2 * r + 2, :]
                dve.wait_ge(s_zs, 4)
                dve.tensor_tensor(z, QB[:, VR2 + 2 * r:VR2 + 2 * r + 2, :], z, ALU.mult).then_inc(s_ry, 1)
                dve.wait_ge(s_ry, 2 * r + 1)
                dve.tensor_tensor(z, z, inv, ALU.mult).then_inc(s_ry, 1)

            def slot2(n):
                if n in (36, 38, 40, 42):
                    decays((n - 36) // 2)
                for r in range(RET_HEADS):
                    step = n - (RET0 + 2 * r)
                    if step == 0:
                        decayed(r)
                    if step == 2:
                        retained(r)
                    if step == 5:
                        gated(r)
                if 0 <= n - (IN2_SLOTS - 8) < 6:
                    converted(n - (IN2_SLOTS - 8), 3 * DT + 6, QB, ZR2, ZA2)
                attention_slot(n, ATT2, 0, 1)
                attention_slot(n, ATT3, 4, 1)

            for n in range(IN2_SLOTS):
                split(B_IN2, LEAD + n)
                slot2(n)
            for s in range(32):
                if s < 28:
                    split(B_OUT2, LEAD + s)
                slot2(IN2_SLOTS + s)
                if s in (13, 15, 23, 31):
                    c = (13, 15, 23, 31).index(s)
                    finished(8 * B_OUT2 + s, G_OUT2 + c)
                    for t in range(4):
                        k = 4 * c + t
                        ins = dve.scalar_tensor_tensor(X[:, k, :], acc_tiles((G_OUT2 + c) % 2)[:, t, :],
                                                       modT[:, 32 + k:33 + k], X[:, k, :], ALU.mult, ALU.add)
                        ins.then_inc(s_tile if c == 3 else s_part, 1)
                    if c < 3:
                        dve.wait_ge(s_part, 4 * c + 4)
                        dve.sem_inc(s_evac, 1)
                    if 0 < c < 3:
                        sum_chunk(3, c, SQX4)
            inverse_root(3)
            dve.wait_ge(s_rb, 4)
            for t in range(DT):
                dve.scalar_tensor_tensor(X[:, t, :], X[:, t, :], col("final", t), rb[:, :], ALU.mult, ALU.mult
                                         ).then_inc(s_fin, 1)

        @block.tensor
        def _(pe):
            def product(b, out, tiles, first, last, hi, lo):
                for half in range(2):
                    kt = tiles[half]
                    for t in range(4):
                        w = slice(512 * half + P * t, 512 * half + P * t + P)
                        pe.matmul(out[:, t, :], whi[:, b, w], hi[:, kt, :], start=first and half == 0 and t % 2 == 0,
                                  stop=False, skip_group_check=True)
                        pe.matmul(out[:, t, :], whi[:, b, w], lo[:, kt, :], start=False, stop=False,
                                  skip_group_check=True)
                        mm = pe.matmul(out[:, t, :], wlo[:, b, w], hi[:, kt, :], start=False, stop=last and half == 1,
                                       skip_group_check=True)
                mm.then_inc(s_used, 1)

            def group(unit, j0, units, grp, par, hi, lo, need):
                pe.wait_ge(s_evac, grp + 1)
                for u in range(units):
                    pe.wait_ge(s_lo, unit + (u + 1))
                    if need is not None:
                        pe.wait_ge(s_gl, need(2 * u + 1))
                    product((j0 + u) % SPLIT, acc_tiles(par), (2 * u, 2 * u + 1), u == 0, u == units - 1, hi, lo)

            def whole(blk, grp, par, need):
                group(blk * 8, 0, 8, grp, par, gh, gl, need)

            def stream_in(blk, grp, n, need):
                g, u = n // 8, n % 8
                if u == 0:
                    pe.wait_ge(s_evac, grp + g + 1)
                pe.wait_ge(s_lo, 8 * blk + n + 1)
                pe.wait_ge(s_gl, need(2 * u + 1))
                product(n % SPLIT, acc_tiles((grp + g) % 2), (2 * u, 2 * u + 1), u == 0, u == 7, gh, gl)

            def stream_out(blk, grp, s, base):
                g, u = OUT_UNITS[s]
                if u == 0:
                    pe.wait_ge(s_evac, grp + g + 1)
                pe.wait_ge(s_lo, 8 * blk + s + 1)
                pe.wait_ge(s_gl, base + (1 + u if u < 6 else 2 * u - 4))
                product(s % SPLIT, acc_tiles((grp + g) % 2), (2 * u, 2 * u + 1), u == 0, u == 7, gh, gl)

            def sum_squares(k, buf):
                pe.wait_ge(s_sum, 2 * k + 2)
                if k:
                    pe.wait_ge(s_root, k)
                for t in range(4):
                    pe.matmul(PS[:, 4, 0:S], ones, buf[:, 0, t, :], start=(t == 0), stop=False)
                for t in range(4):
                    pe.wait_ge(s_sq, 7 * k + 4 + t)
                    mm = pe.matmul(PS[:, 4, 0:S], ones, buf[:, 1, t, :], start=False, stop=(t == 3))
                mm.then_inc(s_ss, 1)

            pe.sem_inc(s_used, SPLIT)
            pe.wait_ge(s_cst, 16)

            def attention(step, h, layer):
                H = layer * HEADS + h
                SB, PTS, VS = (SB2, PTS2, VS2) if layer else (SB1, PTS1, VS1)
                if layer:
                    q, k, v = (QB[:, head_tile(*at_, h), :] for at_ in ((Q02, Q12), (K02, K12), (V02, V12)))
                else:
                    q, k, v = (QKVZ[:, head_tile(*at_, h), :] for at_ in ((Q0, Q1), (K0, K1), (V0, V1)))
                if step == 0:
                    if layer:
                        pe.wait_ge(s_evac, (G_IN2 + 10 if h < 4 else G_IN2 + 13) + 2)
                    else:
                        pe.wait_ge(s_qk, 2 * h + 2)
                    if H >= 1:
                        pe.wait_ge(s_sb, H)
                    for c in range(2):
                        mm = pe.matmul(PS[:, 4, S * c:S * c + S], q[:, P * c:P * c + P], k, start=True, stop=True)
                    mm.then_inc(s_sc, 1)
                if step == 3:
                    if layer:
                        pe.wait_ge(s_evac, (G_IN2 + 11 if h < 4 else G_OUT2) + 2)
                        pe.wait_ge(s_rrt, RET_HEADS)
                    else:
                        pe.wait_ge(s_evac, (G_IN + 8 if h < 4 else G_OUT) + 2)
                        pe.wait_ge(s_nrt, 4 if h < 4 else 8)
                    if H >= 1:
                        pe.wait_ge(s_vs, H)
                    for c in range(2):
                        mm = pe.transpose(PS[:, 7, P * c:P * c + P], v[:, P * c:P * c + P], ident)
                    mm.then_inc(s_vt, 1)
                    pe.wait_ge(s_pn, 2 * H + 2)
                    if H >= 1:
                        pe.wait_ge(s_pts, H)
                    for c in range(2):
                        for b in range(2):
                            mm = pe.transpose(PS[:, 5, S * b + P * c:S * b + P * c + P], SB[:, h % 2, c, P * b:P * b + P],
                                              ident)
                    mm.then_inc(s_pt, 1)
                if step == 5:
                    pe.wait_ge(s_pts, H + 1)
                    pe.wait_ge(s_vs, H + 1)
                    if layer and h:
                        pe.wait_ge(s_gated, h)
                    if not layer and h:
                        pe.wait_ge(s_ahi, h)
                        if h > 4:
                            pe.wait_ge(s_gl, DT + 6 + h - 4)
                    for b in range(2):
                        mm = pe.matmul(PS[:, 6, 0:S], VS[:, h % 2, b, :], PTS[:, h % 2, b, :],
                                       start=(b == 0), stop=(b == 1))
                    mm.then_inc(s_pv, 1)

            def attention_slot(n, b, h0, layer):
                for h in range(h0, h0 + 4):
                    step = n - (b + 2 * (h - h0))
                    if 0 <= step < 6:
                        attention(step, h, layer)

            def slot1(n):
                if n == 5:
                    sum_squares(0, SQX1)
                if n == 9:
                    pe.wait_ge(s_wdtl, 1)
                    for kt in range(DT):
                        w = slice(16 * kt, 16 * kt + P)
                        pe.matmul(PS[:, 5, 0:S], wdt_h[:, w], gh[:, kt, :], start=(kt == 0), stop=False)
                        pe.matmul(PS[:, 5, 0:S], wdt_h[:, w], gl[:, kt, :], start=False, stop=False)
                        mm = pe.matmul(PS[:, 5, 0:S], wdt_l[:, w], gh[:, kt, :], start=False, stop=(kt == DT - 1))
                    mm.then_inc(s_dtp, 1)
                if n == 17:
                    pe.wait_ge(s_la, 1)
                    for k, src in enumerate((W1, W3)):
                        for c in range(2):
                            mm = pe.transpose(PS[:, 5, 32 * k + 16 * c:32 * k + 16 * c + 16], src[0:16, P * c:P * c + P],
                                              ident[0:16, 0:16])
                    mm.then_inc(s_dtr, 1)
                if n == 19:
                    pe.wait_ge(s_dts, 2)
                    for c in range(2):
                        pe.matmul(PS[:, 7, 16 * c:16 * c + 16], tri, LA[:, c, :], start=True, stop=True)
                    pe.matmul(PS[:, 7, 32:48], ones, LA[:, 0, :], start=True, stop=True)
                    for c in range(2):
                        mm = pe.matmul(PS[0:16, 7, S + P * c:S + P * c + P], LA[:, c, :], tri, start=True, stop=True)
                    mm.then_inc(s_ac, 1)
                if 24 <= n < 32:
                    j = n - 24
                    pe.wait_ge(s_silu, 2)
                    if j >= 2:
                        pe.wait_ge(s_xd, 2 * j - 2)
                    for c in range(2):
                        mm = pe.transpose(PS[:, 4 + j % 2, P * c:P * c + P], U[:, j, 3 + P * c:3 + P * c + P], ident)
                    mm.then_inc(s_xt, 1)
                if n in (32, 33):
                    g = n - 32
                    pe.wait_ge(s_silu, 3)
                    if g:
                        pe.wait_ge(s_nb, 1)
                        pe.wait_ge(s_at, 1)
                    bm, cm = U[:, 8 + g, 3:3 + S], U[:, 10 + g, 3:3 + S]
                    pe.matmul(PS[:, 6 + g, 0:S], bm[:, 0:P], cm, start=True, stop=True)
                    pe.matmul(PS[:, 6 + g, S:S + P], bm[:, P:S], cm[:, P:S], start=True, stop=True).then_inc(s_cb, 1)
                if 34 <= n < 34 + SSM_HEADS:
                    h = n - 34
                    pe.wait_ge(s_xd, 16)
                    if h >= 2:
                        pe.wait_ge(s_e, 3 * h - 3)
                    pe.matmul(PS[:, 4 + h % 2, 0:S], ident[0:16, h:h + 1].to_broadcast([16, P]), small[0:16, 256:512],
                              start=True, stop=True).then_inc(s_r, 1)
                if 37 <= n < 37 + SSM_HEADS:
                    q = n - 37
                    lo, bank = 64 * (q % 2), 6 + q // 2 % 2
                    pe.wait_ge(s_m, q + 1)
                    if q >= 4:
                        pe.wait_ge(s_yo, 2 * (q // 2 - 2) + 1)
                    pe.matmul(PS[lo:lo + 64, bank, 0:S], XD[:, 0, 64 * q:64 * q + 64], EM[:, q % 3, 0:2, :],
                              start=True, stop=False, skip_group_check=True)
                    pe.matmul(PS[lo:lo + 64, bank, P:S], XD[:, 1, 64 * q:64 * q + 64], EM[:, q % 3, 2, :],
                              start=False, stop=True, skip_group_check=True).then_inc(s_y, 1)
                if n in (55, 56):
                    g = n - 55
                    pe.wait_ge(s_ysq, g + 1)
                    for t in range(4):
                        mm = pe.matmul(PS[:, 6 + g, 0:S], ones, SQY[g][:, t, :], start=(t == 0), stop=(t == 3))
                    mm.then_inc(s_ysum, 1)
                for b, h0 in ((60, 0), (82, 4)):
                    h, odd = divmod(n - b, 2)
                    if not odd and 0 <= h < 4:
                        h += h0
                        pe.wait_ge(s_nsq, h + 1)
                        if h < 2:
                            pe.wait_ge(s_yrt, 2)
                        if h == 4:
                            pe.wait_ge(s_ahi, 4)
                        if h >= 2:
                            pe.wait_ge(s_nrt, h - 1)
                        pe.matmul(PS[:, 6 + h % 2, :], ones, PTS1[:, h % 2, :, :], start=True, stop=True).then_inc(s_nr, 1)
                attention_slot(n, ATT0, 0, 0)
                attention_slot(n, ATT1, 4, 0)

            W1, W3 = DTW[:, 1, :], DTW[:, 3, :]
            LA = small[:, 88:120].rearrange("p (c h) -> p c h", c=2)
            for n in range(IN_SLOTS):
                stream_in(B_IN, G_IN, n, lambda kt: kt + 1)
                slot1(n)
            for s in range(32):
                stream_out(B_OUT, G_OUT, s, DT)
                slot1(IN_SLOTS + s)
            need_ff = lambda kt: DT + 10 + kt + 1
            whole(B_FF, G_FF, G_FF % 2, need_ff)
            sum_squares(1, SQX2)
            whole(B_FF + 1, G_FF + 1, (G_FF + 1) % 2, need_ff)

            def down(i, unit, grp, hi=ah, lo=al):
                pe.wait_ge(s_al, i + 1)
                for d in range(4):
                    group(unit + 2 * d, 2 * d, 2, grp + d, (G_FF + d) % 2, hi, lo, None)

            with pe.Fori(1, FF_GROUPS) as i:
                whole(i * 3 + (B_FF - 1), i * 6 + (G_FF - 4), G_FF % 2, need_ff)
                whole(i * 3 + B_FF, i * 6 + (G_FF - 3), (G_FF + 1) % 2, need_ff)
                down(i - 1, i * 24 + 8 * (B_FF + 1), i * 6 + (G_FF - 2))
            pe.wait_ge(s_tr, 24)
            for b in range(4):
                mm = pe.matmul(PS[32 * b:32 * b + 32, 5, 0:48], ident32, RQ[:, b::4], start=True, stop=True)
            mm.then_inc(s_mod, 1)
            down(FF_GROUPS - 1, 8 * (B_IN2 - 1), G_IN2 - 4, ah2, al2)
            sum_squares(2, SQX2)

            def slot2(n):
                for r in range(RET_HEADS):
                    step = n - (RET0 + 2 * r)
                    if step == 0:
                        pe.wait_ge(s_evac, G_IN2 + 8 + 2)
                        if r:
                            pe.wait_ge(s_rvs, r)
                            pe.wait_ge(s_rm, r)
                        for c in range(2):
                            for e in range(2):
                                mm = pe.transpose(PS[:, 4, S * c + P * e:S * c + P * e + P],
                                                  QB[:, VR2 + 2 * r + e, P * c:P * c + P], ident)
                        mm.then_inc(s_rvt, 1)
                        for c in range(2):
                            mm = pe.matmul(PS[:, 5, S * c:S * c + S], QB[:, KR2 + r, P * c:P * c + P], QB[:, QR2 + r, :],
                                           start=True, stop=True)
                        mm.then_inc(s_rsc, 1)
                    if step == 2:
                        pe.wait_ge(s_rm, r + 1)
                        pe.wait_ge(s_rvs, r + 1)
                        if r:
                            pe.wait_ge(s_or, r)
                        for e in range(2):
                            for c in range(2):
                                mm = pe.matmul(PS[:, 6, S * e:S * e + S], PTS2[:, r % 2, c, P * e:P * e + P],
                                               SB2[:, r % 2, c, :], start=(c == 0), stop=(c == 1))
                        mm.then_inc(s_ro, 1)
                    if step == 5:
                        pe.wait_ge(s_rsq, r + 1)
                        if r:
                            pe.wait_ge(s_rrt, r)
                        for e in range(2):
                            mm = pe.matmul(PS[:, 7, 0:S], ones, SQR[:, r % 2, e, :], start=(e == 0), stop=(e == 1))
                        mm.then_inc(s_rsum, 1)
                attention_slot(n, ATT2, 0, 1)
                attention_slot(n, ATT3, 4, 1)

            before = 2 * DT + 10
            for n in range(IN2_SLOTS):
                stream_in(B_IN2, G_IN2, n, lambda kt: before + kt + 1)
                slot2(n)
            for s in range(32):
                stream_out(B_OUT2, G_OUT2, s, before + DT)
                slot2(IN2_SLOTS + s)
            sum_squares(3, SQX4)


def _units(w):
    k, n = w.shape
    return w.reshape(k // 256, 2, P, n // 512, 512).transpose(3, 0, 2, 1, 4).reshape(n // 512, k // 256, P, 1024)


def _out_units(w):
    u = _units(w)
    return [u[g, OUT_TILES[2 * k] // 2][None] for g, k in OUT_UNITS]


def _cols(v):
    return v.reshape(-1, P).T


def kernel(**inputs):
    import numpy as np
    import concourse.bacc as bacc
    from concourse.bass_utils import run_bass_kernel_spmd

    a = {k: np.asarray(v) for k, v in inputs.items()}
    f = np.float32
    w_in = a["w_in"][0]
    gates = _units(a["w_up"][0])
    downs = _units(a["w_down"][0])
    xbc, qkvz = _units(w_in[:, 4096:5632]), _units(w_in[:, :4096])
    parts = [xbc] + [qkvz[g] for g in (6, 7, 0, 2, 4, 1, 3, 5)] + _out_units(a["w_out"][0])
    for i in range(FF_GROUPS + 1):
        if i < FF_GROUPS:
            parts += [gates[i], gates[FF_GROUPS + i]]
        if i:
            parts.append(downs[:, 2 * i - 2:2 * i])
    mix2 = _units(a["w_in_2"][0])
    parts += [mix2[g] for g in (6, 7, 12, 13, 8, 9, 10, 11, 0, 2, 4, 1, 3, 5)] + _out_units(a["w_out_2"][0])
    weights = np.concatenate([p.reshape(-1, P, 1024) for p in parts])
    assert len(weights) == BLOCKS * RAW
    w_dt = np.concatenate([w_in[:, 5632:].reshape(DT, P, 16).transpose(1, 0, 2).reshape(P, -1), np.zeros((P, 112), f)],
                          axis=1)
    w_ada = a["w_ada_2"][0].reshape(DT, P, ADA_CHUNKS, ADA_CHUNK).transpose(2, 0, 1, 3).reshape(-1, P, ADA_CHUNK)

    def rows(v):
        return np.broadcast_to(v.reshape(1, -1), (P, v.size))

    ssm_conv = np.stack([_cols(a["ssm_conv_b"][0])] + [_cols(w) for w in a["ssm_conv_w"][0]], axis=2).reshape(P, -1)
    ffn_conv = np.stack([_cols(a["ffn_conv_b"][0])] + [_cols(w) for w in a["ffn_conv_w"][0]], axis=2).reshape(P, -1)
    table = dict(norm1=_cols(a["norm1_w"][0]), norm2=_cols(a["norm2_w"][0]), ssm_norm=_cols(a["ssm_norm_w"][0]),
                 q_norm=_cols(a["q_norm_w"][0]), k_norm=_cols(a["k_norm_w"][0]), gain2=_cols(a["norm_gain_2"][0]),
                 final=_cols(a["final_gain_2"]), c=_cols(a["c_2"][0]), b_ada=_cols(a["b_ada_2"][0]),
                 d_skip=_cols(np.repeat(a["d_skip"][0], 64)), ssm_conv=ssm_conv, ffn_conv=ffn_conv,
                 dt_bias=np.pad(a["dt_bias"][0], (0, P - 16))[:, None], a_log=np.pad(a["a_log"][0], (0, P - 16))[:, None],
                 decay=np.concatenate([rows(a["ret_decay_logit_f_2"][0]), rows(a["ret_decay_logit_b_2"][0])], axis=1),
                 eps=np.full((P, 1), EPS, f))
    params = np.concatenate([table[k] for k in COLS], axis=1)
    xT = a["x"][0].T.reshape(DT, P, S).transpose(1, 0, 2)
    i, j = np.arange(P)[:, None], np.arange(P)[None, :]
    row = (np.arange(P)[:, None, None] + P * np.arange(2)[None, :, None])
    column = np.arange(S)[None, None, :]
    causal = np.where(column <= row, 0.0, -3e38)
    const1 = np.concatenate([np.ones((P, P)), i == j, i <= j, i % 32 == j[:, 0:32], causal.reshape(P, -1)], axis=1).astype(f)
    dist = np.abs(row - column)
    windows = (dist <= 64) * 1 + (dist % 4 == 0) + (dist % 16 == 0)
    log_windows = np.where(windows > 0, np.log(np.maximum(windows, 1)), -1e30)
    behind, ahead = np.maximum(column - row, 0), np.maximum(row - column, 0)
    const2 = np.stack([dist, log_windows, behind, ahead, column >= row, column <= row], axis=1).astype(f)

    nc = bacc.Bacc("TRN2", target_bir_lowering=False, num_devices=1)
    arrays, args = {}, []
    for name, v in dict(xT=xT, weights=weights, w_dt=w_dt, w_ada=w_ada, params=params, const1=const1,
                        const2=const2).items():
        arrays[name] = np.ascontiguousarray(v)
        args.append(nc.dram_tensor(name, v.shape, mybir.dt.from_np(arrays[name].dtype), kind="ExternalInput").ap())
    outT = nc.dram_tensor("outT", (P, DT, S), F32, kind="ExternalOutput").ap()
    build(nc, *args, outT)
    r = run_bass_kernel_spmd(nc, [arrays], core_ids=[0])
    out = r.results[0]["outT"]
    return out.transpose(1, 0, 2).reshape(1, D, S).transpose(0, 2, 1)
```
